# Optimizing a Trainium2 kernel written in Bass

```python
import jax, jax.numpy as jnp
from jax import lax
import numpy as np

D_MODEL = 1024
BATCH = 1
SEQ = 256
DEPTH = 1
DEC_BATCH = 1
DEC_SEQ = 2048
PAST_LEN = 512

GRID_W = 64
HGRN_HEADS = 4
HEAD_K = 128
HEAD_V = 128
HGRN_WIDTH = HGRN_HEADS * HEAD_V
POOL_WINDOWS = (2, 4, 8, 16)
POOL_GROUP = 128
POOL_WIDTH = len(POOL_WINDOWS) * POOL_GROUP
CHUNK = 32
N_EXPERTS = 32
TOP_K = 4
D_FF = D_MODEL
SWIGLU_LIMIT = 7.0
SWIGLU_ALPHA = 1.702
EPS = 1e-6
IN_WIDTH = 5 * HGRN_WIDTH + POOL_WIDTH + 2 * D_MODEL
IN_SPLITS = (HGRN_WIDTH, 2 * HGRN_WIDTH, 3 * HGRN_WIDTH, 4 * HGRN_WIDTH, 5 * HGRN_WIDTH,
             5 * HGRN_WIDTH + POOL_WIDTH, 5 * HGRN_WIDTH + POOL_WIDTH + D_MODEL)

kernel_name = 'hgrn2_pool_moe_flow_step'

def rms_norm(x, g):
    xf = x.astype(jnp.float32)
    y = xf * lax.rsqrt(jnp.mean(xf * xf, axis=-1, keepdims=True) + EPS)
    return (y * g.astype(jnp.float32)).astype(x.dtype)

def gla_chunk_scan(q, k, v, g, s0):
    b_, h_, L, _ = q.shape
    n = L // CHUNK

    def chunks(a):
        return a.reshape(b_, h_, n, CHUNK, a.shape[-1]).transpose(2, 0, 1, 3, 4)

    lower = jnp.tril(jnp.ones((CHUNK, CHUNK), dtype=bool))[:, :, None]

    def step(S, inp):
        qc, kc, vc, gc = inp
        cum = jnp.cumsum(gc, axis=2)
        diff = cum[:, :, :, None, :] - cum[:, :, None, :, :]
        decay = jnp.exp(jnp.where(lower, diff, -jnp.inf))
        scores = jnp.einsum('bhtk,bhtsk,bhsk->bhts', qc, decay, kc)
        o = (jnp.einsum('bhts,bhsv->bhtv', scores, vc)
             + jnp.einsum('bhtk,bhkv->bhtv', qc * jnp.exp(cum), S))
        last = cum[:, :, -1:, :]
        S = (jnp.exp(last[:, :, 0, :])[..., None] * S
             + jnp.einsum('bhsk,bhsv->bhkv', kc * jnp.exp(last - cum), vc))
        return S, o

    s_fin, o = lax.scan(step, s0, (chunks(q), chunks(k), chunks(v), chunks(g)))
    return o.transpose(1, 2, 0, 3, 4).reshape(b_, h_, L, -1), s_fin

def hgrn2_mixer(q, f_fwd, f_bwd, iv, og, lb, norm_g, s0):
    B, L, _ = q.shape

    def heads(a):
        return a.reshape(B, L, HGRN_HEADS, -1).transpose(0, 2, 1, 3).astype(jnp.float32)

    qh = heads(q) * (HEAD_K ** -0.5)
    vh = heads(iv)
    s0f = s0.astype(jnp.float32)

    def direction(fz, lbd, s_init, rev):
        f = lbd + (1.0 - lbd) * jax.nn.sigmoid(fz.astype(jnp.float32))
        fh = heads(f)
        qd, kd, vd, gd = qh, 1.0 - fh, vh, jnp.log(fh)
        if rev:
            qd, kd, vd, gd = (jnp.flip(a, axis=2) for a in (qd, kd, vd, gd))
        o, s_fin = gla_chunk_scan(qd, kd, vd, gd, s_init)
        if rev:
            o = jnp.flip(o, axis=2)
        return o, s_fin

    o_f, s_f = direction(f_fwd, lb[0], s0f[:, 0], False)
    o_b, s_b = direction(f_bwd, lb[1], s0f[:, 1], True)
    o = (o_f + o_b).transpose(0, 2, 1, 3)
    o = rms_norm(o, norm_g).reshape(B, L, HGRN_WIDTH) * jax.nn.silu(og.astype(jnp.float32))
    return o.astype(q.dtype), jnp.stack([s_f, s_b], axis=1).astype(q.dtype)

def window_mean(u, w, axis):
    L = u.shape[axis]
    pos = jnp.arange(L)
    lo = jnp.clip(pos - w // 2, 0, L - 1)
    hi = jnp.clip(pos - w // 2 + w - 1, 0, L - 1)
    cs = jnp.cumsum(u.astype(jnp.float32), axis=axis)
    cs = jnp.concatenate([jnp.zeros_like(lax.slice_in_dim(cs, 0, 1, axis=axis)), cs], axis=axis)
    s = jnp.take(cs, hi + 1, axis=axis) - jnp.take(cs, lo, axis=axis)
    shape = [1] * u.ndim
    shape[axis] = L
    cnt = (hi - lo + 1).astype(jnp.float32).reshape(shape)
    return (s / cnt).astype(u.dtype)

def pool_mixer(u, w_pool, pool_scale, grid):
    B, L, _ = u.shape
    outs = []
    for g, w in enumerate(POOL_WINDOWS):
        ug = u[..., g * POOL_GROUP:(g + 1) * POOL_GROUP]
        if grid:
            rows = L // GRID_W
            ug2 = ug.reshape(B, rows, GRID_W, POOL_GROUP)
            pm = window_mean(window_mean(ug2, w, 1), w, 2).reshape(B, L, POOL_GROUP)
        else:
            pm = window_mean(ug, w, 1)
        outs.append(jnp.einsum('blc,cd->bld', pm - ug, w_pool[g]))
    return jnp.concatenate(outs, axis=-1) * pool_scale

def moe_ffn(h, w_router, b_router, w_gate_up, b_gate_up, w_down, b_down):
    B, L, D = h.shape
    T = B * L
    hf = h.reshape(T, D)
    logits = (hf @ w_router + b_router).astype(jnp.float32)
    top_v, top_i = lax.top_k(logits, TOP_K)
    wts = jax.nn.softmax(top_v, axis=-1)
    flat_e = top_i.reshape(-1)
    order = jnp.argsort(flat_e)
    tok = order // TOP_K
    e_sorted = flat_e[order]
    sizes = jnp.bincount(flat_e, length=N_EXPERTS).astype(jnp.int32)
    xs = hf[tok]
    gu = lax.ragged_dot(xs, w_gate_up, sizes) + b_gate_up[e_sorted]
    gate = jnp.minimum(gu[:, :D_FF].astype(jnp.float32), SWIGLU_LIMIT)
    up = jnp.clip(gu[:, D_FF:].astype(jnp.float32), -SWIGLU_LIMIT, SWIGLU_LIMIT)
    act = ((up + 1.0) * gate * jax.nn.sigmoid(SWIGLU_ALPHA * gate)).astype(h.dtype)
    out = lax.ragged_dot(act, w_down, sizes) + b_down[e_sorted]
    out = out.astype(jnp.float32) * wts.reshape(-1)[order][:, None]
    y = jax.ops.segment_sum(out, tok, num_segments=T)
    return y.reshape(B, L, D).astype(h.dtype)

def trunk_layer(x, mod, s0, grid, w_in, lb, hgrn_norm, w_pool, pool_scale, w_branch_a, w_branch_b,
                w_out, norm1, norm2, w_router, b_router, w_gate_up, b_gate_up, w_down, b_down):
    shift1, scale1, gate1, shift2, scale2, gate2 = jnp.split(mod, 6, axis=-1)
    h = rms_norm(x, norm1) * (1 + scale1) + shift1
    q, f_fwd, f_bwd, iv, og, pu, ga, gb = jnp.split(h @ w_in, IN_SPLITS, axis=-1)
    y_a, s_fin = hgrn2_mixer(q, f_fwd, f_bwd, iv, og, lb, hgrn_norm, s0)
    y_b = pool_mixer(pu, w_pool, pool_scale, grid)
    merged = jax.nn.sigmoid(ga) * (y_a @ w_branch_a) + jax.nn.sigmoid(gb) * (y_b @ w_branch_b)
    x = x + gate1 * (merged @ w_out)
    h2 = rms_norm(x, norm2) * (1 + scale2) + shift2
    x = x + gate2 * moe_ffn(h2, w_router, b_router, w_gate_up, b_gate_up, w_down, b_down)
    return x, s_fin

def setup_inputs(seed: int = 0) -> dict:
    key = jax.random.key(seed)
    ks = jax.random.split(key, 24)
    D = D_MODEL

    def nrm(k, shape, s):
        return jax.random.normal(k, shape, jnp.float32) * s

    return {
        'x_prompt': nrm(ks[0], (BATCH, SEQ, D), 1.0),
        'x_sample': nrm(ks[1], (DEC_BATCH, DEC_SEQ, D), 1.0),
        'state_hgrn': nrm(ks[2], (DEC_BATCH, DEPTH, 2, HGRN_HEADS, HEAD_K, HEAD_V), 0.5),
        'c': nrm(ks[3], (DEC_BATCH, D), 1.0),
        'c_ctx': nrm(ks[4], (D,), 1.0),
        'w_ada': nrm(ks[5], (DEPTH, D, 6 * D), 0.5 * D ** -0.5),
        'b_ada': nrm(ks[6], (DEPTH, 6 * D), 0.02),
        'norm1': 1.0 + nrm(ks[7], (DEPTH, D), 0.05),
        'w_in': nrm(ks[8], (DEPTH, D, IN_WIDTH), D ** -0.5),
        'hgrn_lb': nrm(ks[9], (DEPTH + 1, 2, HGRN_WIDTH), 0.5),
        'hgrn_norm': 1.0 + nrm(ks[10], (DEPTH, HEAD_V), 0.05),
        'w_pool': nrm(ks[11], (DEPTH, len(POOL_WINDOWS), POOL_GROUP, POOL_GROUP), POOL_GROUP ** -0.5),
        'pool_scale': 1.0 + nrm(ks[12], (DEPTH, POOL_WIDTH), 0.1),
        'w_branch_a': nrm(ks[13], (DEPTH, HGRN_WIDTH, D), HGRN_WIDTH ** -0.5),
        'w_branch_b': nrm(ks[14], (DEPTH, POOL_WIDTH, D), POOL_WIDTH ** -0.5),
        'w_out': nrm(ks[15], (DEPTH, D, D), D ** -0.5),
        'norm2': 1.0 + nrm(ks[16], (DEPTH, D), 0.05),
        'w_router': nrm(ks[17], (DEPTH, D, N_EXPERTS), D ** -0.5),
        'b_router': nrm(ks[18], (DEPTH, N_EXPERTS), 0.01),
        'w_gate_up': nrm(ks[19], (DEPTH, N_EXPERTS, D, 2 * D_FF), D ** -0.5),
        'b_gate_up': nrm(ks[20], (DEPTH, N_EXPERTS, 2 * D_FF), 0.02),
        'w_down': nrm(ks[21], (DEPTH, N_EXPERTS, D_FF, D), D_FF ** -0.5),
        'b_down': nrm(ks[22], (DEPTH, N_EXPERTS, D), 0.02),
        'final_norm': 1.0 + nrm(ks[23], (D,), 0.05),
    }

def reference(x_prompt, x_sample, state_hgrn, c, c_ctx, w_ada, b_ada, norm1, w_in, hgrn_lb, hgrn_norm,
              w_pool, pool_scale, w_branch_a, w_branch_b, w_out, norm2, w_router, b_router,
              w_gate_up, b_gate_up, w_down, b_down, final_norm):
    lb_all = jnp.cumsum(jax.nn.softmax(hgrn_lb.astype(jnp.float32), axis=0), axis=0)
    xp, xs = x_prompt, x_sample
    zero_state = jnp.zeros((x_prompt.shape[0], 2, HGRN_HEADS, HEAD_K, HEAD_V), jnp.float32)
    ctx_states = []
    for l in range(DEPTH):
        weights = (w_in[l], lb_all[l], hgrn_norm[l], w_pool[l], pool_scale[l], w_branch_a[l],
                   w_branch_b[l], w_out[l], norm1[l], norm2[l], w_router[l], b_router[l],
                   w_gate_up[l], b_gate_up[l], w_down[l], b_down[l])
        mod_ctx = (jax.nn.silu(c_ctx) @ w_ada[l] + b_ada[l])[None, None, :]
        mod_lat = (jax.nn.silu(c) @ w_ada[l] + b_ada[l])[:, None, :]
        xp, s_ctx = trunk_layer(xp, mod_ctx, zero_state, False, *weights)
        xs, _ = trunk_layer(xs, mod_lat, state_hgrn[:, l], True, *weights)
        ctx_states.append(s_ctx)
    y_prompt = rms_norm(xp, final_norm)
    y_sample = rms_norm(xs, final_norm)
    new_state_hgrn = jnp.stack(ctx_states, axis=1)
    return (y_prompt, y_sample, new_state_hgrn)


_drawn_inputs = setup_inputs


def setup_inputs(seed=0):
    import zlib

    import numpy as np

    out = dict(_drawn_inputs(seed))
    spreads = {}
    factors = {'state_hgrn': 8.0,
     'hgrn_norm': 5.344,
     'pool_scale': 2.844,
     'b_router': 5.243,
     'b_gate_up': 8.0,
     'b_down': 8.0}
    for name, (base, spread) in spreads.items():
        noise = np.random.default_rng([zlib.crc32(name.encode()), seed]).standard_normal(out[name].shape)
        drawn = base * np.exp(spread * noise) if base else spread * noise
        out[name] = __import__('jax').numpy.asarray(drawn.astype(out[name].dtype))
    for name, factor in factors.items():
        out[name] = (out[name] * factor).astype(out[name].dtype)
    return out
```

```python
from contextlib import ExitStack

import numpy as np

import concourse.bass as bass
import concourse.mybir as mybir
from concourse.alu_op_type import AluOpType as ALU

ACT = mybir.ActivationFunctionType
AX = mybir.AxisListType
F32 = mybir.dt.float32
F16 = mybir.dt.float16
I32 = mybir.dt.int32
U32 = mybir.dt.uint32

P = 128
D = 1024
KD = D // P
CTX, LAT = 256, 2048
T = CTX + LAT
NT = T // P
HEADS = 4
CHUNK = 32
CPT = P // CHUNK
NCOL = 5120 // P
E = 32
TOPK = 4
GRID_W = 64
GRID_H = LAT // GRID_W
WINDOWS = (2, 4, 8, 16)
EPS = 1e-6
LIMIT = 7.0
ALPHA = 1.702
X_SCALE = 16.0
W_SCALE = 256.0
DESCALE = 1.0 / (X_SCALE * W_SCALE)
MAX_BLOCKS = TOPK * T // P + E
MAX_PER_EXPERT = NT

GROUPS = [(0, CTX)] + [(CTX + 512 * g, 512) for g in range(LAT // 512)]


def stage_modulation(nc, io, keep):
    with ExitStack() as ctx:
        sb = lambda n, s, d=F32: ctx.enter_context(nc.sbuf_tensor(n, s, d))
        ps = lambda n, s: ctx.enter_context(nc.psum_tensor(n, s, F32))
        sem = nc.alloc_semaphore
        CB = 512
        NB = 6 * D // CB
        MB = CB // P
        w = sb("m_w", [P, 2, KD, CB])
        cc = sb("m_cc", [P, KD, 2])
        sc = sb("m_sc", [P, KD, 2])
        b_ada = sb("m_bada", [P, 48])
        n1 = sb("m_n1", [P, KD])
        n2 = sb("m_n2", [P, KD])
        ident = sb("m_ident", [P, P])
        modc = sb("m_modc", [P, 2, 48])
        modr = sb("m_modr", [P, 2, 4, KD])
        rows = sb("m_rows", [64, P])
        lbz = sb("m_lbz", [P, 2, 8])
        lbt = sb("m_lbt", [P, 4, 8])
        pm = ps("m_pm", [P, 2, 512])
        pt = ps("m_pt", [P, 512])
        small_in, silu_in, w_in = sem("m_small_in"), sem("m_silu"), [sem(f"m_w_in{u}") for u in range(2)]
        mod_ready, mod_used = sem("m_mod_ready"), sem("m_mod_used")
        rows_in, rows_t, rows_sb, rows_out = sem("m_rows_in"), sem("m_rows_t"), sem("m_rows_sb"), sem("m_rows_out")
        lb_e, lb_m = sem("m_lb_e"), sem("m_lb_m")
        A1, B1, lb, oml = keep["A1"], keep["B1"], keep["lb"], keep["oml"]
        w_v = io["w_ada"].rearrange("(k p) n -> p k n", p=P)
        with nc.Block() as block:

            @block.sync
            def _(sp):
                for dst, src in ((cc, "cc"), (b_ada, "b_ada_c"), (n1, "norm1_c"), (n2, "norm2_c"),
                                 (ident, "ident"), (lbz, "lb_c")):
                    sp.dma_start(dst[:], io[src]).then_inc(small_in, 16)
                with sp.Fori(0, NB // 2) as i:
                    for u in range(2):
                        sp.wait_ge(mod_ready, i * 2 + u + 1)
                        sp.dma_start(w[:, u], w_v[:, :, bass.ts(i * 2 + u, CB)]).then_inc(w_in[u], 16)
                sp.wait_ge(rows_sb, 1)
                sp.dma_start(io["mod_rows"], rows[:]).then_inc(rows_out, 16)
                sp.wait_ge(rows_out, 16)

            @block.scalar
            def _(act):
                act.wait_ge(small_in, 96)
                nc.scalar.activation(sc[:], cc[:], ACT.Sigmoid).then_inc(silu_in, 1)
                act.wait_ge(lb_m, 1)
                nc.scalar.activation(lbt[:, 0], lbt[:, 2], ACT.Exp)
                nc.scalar.activation(lbt[:, 1], lbt[:, 3], ACT.Exp).then_inc(lb_e, 1)

            @block.tensor
            def _(pe):
                pe.sem_inc(mod_ready, 2)
                pe.wait_ge(silu_in, 2)
                with pe.Fori(0, NB // 2) as i:
                    for u in range(2):
                        pe.wait_ge(w_in[u], i * 16 + 16)
                        pe.wait_ge(mod_used, i * 2 + u + 1)
                        for m in range(MB):
                            for k in range(KD):
                                mm = nc.tensor.matmul(pm[:, u, 2 * m:2 * m + 2], w[:, u, k, bass.ts(m, P)],
                                                      sc[:, k], start=(k == 0), stop=(k == KD - 1))
                        mm.then_inc(mod_ready, 1)
                pe.wait_ge(rows_in, 1)
                nc.tensor.transpose(pt[0:64, 0:P], modr[:].rearrange("p v q k -> p (v q k)"), ident[:]).then_inc(rows_t, 1)

            @block.vector
            def _(dve):
                dve.sem_inc(mod_used, 2)
                dve.wait_ge(silu_in, 1)
                nc.vector.tensor_tensor(sc[:], sc[:], cc[:], ALU.mult).then_inc(silu_in, 1)
                nc.vector.tensor_tensor(lb[:], lbz[:, 0], lbz[:, 1], ALU.max)
                dve.drain()
                nc.vector.tensor_tensor(lbt[:, 2], lbz[:, 0], lb[:], ALU.subtract)
                nc.vector.tensor_tensor(lbt[:, 3], lbz[:, 1], lb[:], ALU.subtract).then_inc(lb_m, 1)
                dve.wait_ge(lb_e, 1)
                nc.vector.tensor_tensor(lbt[:, 1], lbt[:, 0], lbt[:, 1], ALU.add)
                dve.drain()
                nc.vector.reciprocal(lbt[:, 2], lbt[:, 1])
                dve.drain()
                nc.vector.tensor_tensor(lb[:], lbt[:, 0], lbt[:, 2], ALU.mult)
                dve.drain()
                nc.vector.tensor_scalar(oml[:], lb[:], -1.0, 1.0, ALU.mult, ALU.add)
                with dve.Fori(0, NB // 2) as i:
                    for u in range(2):
                        dve.wait_ge(mod_ready, i * 2 + u + 3)
                        for v in range(2):
                            ins = nc.vector.tensor_tensor(
                                modc[:, v, bass.ts(i * 2 + u, MB)],
                                pm[:, u, 0:2 * MB].rearrange("p (m v) -> p v m", v=2)[:, v],
                                b_ada[:, bass.ts(i * 2 + u, MB)], ALU.add)
                        ins.then_inc(mod_used, 1)
                dve.drain()
                for v in range(2):
                    m = lambda q: modc[:, v, q * KD:(q + 1) * KD]
                    nc.vector.tensor_scalar(B1[:, v], m(0), X_SCALE, None, ALU.mult)
                    nc.vector.scalar_tensor_tensor(A1[:, v], m(1), 1.0, n1[:], ALU.add, ALU.mult)
                    nc.vector.tensor_scalar(modr[:, v, 0], m(2), DESCALE, None, ALU.mult)
                    nc.vector.tensor_scalar(modr[:, v, 2], m(3), X_SCALE, None, ALU.mult)
                    nc.vector.scalar_tensor_tensor(modr[:, v, 1], m(4), 1.0, n2[:], ALU.add, ALU.mult)
                    nc.vector.tensor_copy(modr[:, v, 3], m(5))
                dve.drain()
                nc.vector.tensor_scalar(A1[:], A1[:], X_SCALE, None, ALU.mult)
                nc.vector.tensor_scalar(modr[:, :, 1], modr[:, :, 1], X_SCALE, None, ALU.mult).then_inc(rows_in, 1)
                dve.wait_ge(rows_t, 1)
                nc.vector.tensor_copy(rows[:], pt[0:64, 0:P]).then_inc(rows_sb, 1)


def stage_normed(nc, io, keep):
    with ExitStack() as ctx:
        sb = lambda n, s, d=F32: ctx.enter_context(nc.sbuf_tensor(n, s, d))
        ps = lambda n, s: ctx.enter_context(nc.psum_tensor(n, s, F32))
        sem = nc.alloc_semaphore
        ident = sb("n_ident", [P, P])
        x = sb("n_x", [P, 2, D])
        xn = sb("n_xn", [P, 2, D])
        sq = sb("n_sq", [P, D])
        ss = sb("n_ss", [P, 2])
        ms = sb("n_ms", [P, 2])
        rstd = sb("n_rstd", [P, 2])
        mhalf = sb("n_mhalf", [P, 1])
        h = sb("n_h", [P, 2, KD, P])
        pt = ps("n_pt", [P, 2, D])
        id_in, x_in, rms_ready = sem("n_id_in"), [sem(f"n_x_in{u}") for u in range(2)], sem("n_rms_ready")
        ss_ready = sem("n_ss_ready")
        tick = sem("n_tick")
        xn_ready, t_ready, h_ready, hi_ready, h_used = (sem("n_xn_ready"), sem("n_t_ready"), sem("n_h_ready"),
                                                        sem("n_hi_ready"), sem("n_h_used"))
        hi, lo = keep["hT_hi"], keep["hT_lo"]
        A1, B1 = keep["A1"], keep["B1"]

        def tiles(eng, body):
            body(0, 0)
            with eng.Fori(1, NT // 2) as i:
                body(1, i)

        with nc.Block() as block:

            @block.sync
            def _(sp):
                sp.dma_start(ident[:], io["ident"]).then_inc(id_in, 16)

                def body(v, i):
                    for u in range(2):
                        sp.wait_ge(xn_ready, i * 2 + u + 1)
                        sp.dma_start(x[:, u], io["x"][bass.ts(i * 2 + u, P), :]).then_inc(x_in[u], 16)
                tiles(sp, body)

            @block.scalar
            def _(act):
                def body(v, i):
                    for u in range(2):
                        act.wait_ge(x_in[u], i * 16 + 16)
                        act.wait_ge(rms_ready, i * 2 + u + 1)
                        nc.scalar.activation(sq[:], x[:, u], ACT.Square, accum_out=ss[:, u:u + 1]).then_inc(ss_ready, 1)
                        act.drain()
                    for u in range(2):
                        act.wait_ge(h_ready, i * 2 + u + 1)
                        nc.scalar.copy(hi[:, :, bass.ts(i * 2 + u, P)], h[:, u]).then_inc(hi_ready, 1)
                tiles(act, body)

            @block.gpsimd
            def _(pool):
                nc.gpsimd.memset(mhalf[:], -0.5)
                pool.drain()
                pool.sem_inc(rms_ready, 2)

                def body(v, i):
                    for u in range(2):
                        pool.wait_ge(ss_ready, i * 2 + u + 1)
                        pool.wait_ge(xn_ready, i * 2 + u + 1)
                        pool.sem_inc(tick, 1)
                        nc.gpsimd.tensor_scalar(ms[:, u:u + 1], ss[:, u:u + 1], 1.0 / D, EPS, ALU.mult, ALU.add)
                        pool.drain()
                        nc.gpsimd.tensor_tensor(rstd[:, u:u + 1], ms[:, u:u + 1], mhalf[:], ALU.pow).then_inc(rms_ready, 1)
                tiles(pool, body)

            @block.vector
            def _(dve):
                dve.sem_inc(xn_ready, 2)

                def body(v, i):
                    for u in range(2):
                        dve.wait_ge(rms_ready, i * 2 + u + 3)
                        dve.wait_ge(t_ready, i * 2 + u + 1)
                        nc.vector.tensor_scalar(xn[:, u], x[:, u], rstd[:, u:u + 1], None, ALU.mult).then_inc(xn_ready, 1)
                    for u in range(2):
                        dve.wait_ge(t_ready, i * 2 + u + 3)
                        dve.wait_ge(hi_ready, i * 2 + u + 1)
                        for j in range(KD):
                            ins = nc.vector.tensor_scalar(h[:, u, j], pt[:, u, bass.ts(j, P)], A1[:, v, j:j + 1],
                                                          B1[:, v, j:j + 1], ALU.mult, ALU.add)
                        ins.then_inc(h_ready, 1)
                    for u in range(2):
                        dve.wait_ge(hi_ready, i * 2 + u + 3)
                        nc.vector.tensor_tensor(lo[:, :, bass.ts(i * 2 + u, P)], h[:, u],
                                                hi[:, :, bass.ts(i * 2 + u, P)], ALU.subtract).then_inc(h_used, 1)
                    dve.drain()
                dve.sem_inc(hi_ready, 2)
                tiles(dve, body)

            @block.tensor
            def _(pe):
                pe.sem_inc(t_ready, 2)
                pe.wait_ge(id_in, 16)

                def body(v, i):
                    for u in range(2):
                        pe.wait_ge(xn_ready, i * 2 + u + 3)
                        if v:
                            pe.wait_ge(h_ready, i * 2 + u - 1)
                        for j in range(KD):
                            mm = nc.tensor.transpose(pt[:, u, bass.ts(j, P)], xn[:, u, bass.ts(j, P)], ident[:])
                        mm.then_inc(t_ready, 1)
                tiles(pe, body)


Q0, F0, OG0, PU0, GATE0, IV0 = 0, 4, 12, 16, 20, 36


def stage_projection(nc, io, keep):
    with ExitStack() as ctx:
        sb = lambda n, s, d=F32: ctx.enter_context(nc.sbuf_tensor(n, s, d))
        sem = nc.alloc_semaphore
        raw = sb("p_raw", [P, 4, KD, P])
        wh = sb("p_wh", [P, 4, KD, P], F16)
        wl = sb("p_wl", [P, 4, KD, P], F16)
        ob = sb("p_ob", [P, 2, T])
        sg = sb("p_sg", [P, 2, T])
        acc = ctx.enter_context(nc.psum_tensor("p_acc", [P, 8, 512], F32))
        raw_in, wh_ready, wl_ready = [sem(f"p_raw_in{u}") for u in range(2)], sem("p_wh_ready"), sem("p_wl_ready")
        acc_ready, acc_used = sem("p_acc_ready"), sem("p_acc_used")
        f_sig, f_ready, ob_ready, ob_out = (sem("p_f_sig"), sem("p_f_ready"), sem("p_ob_ready"),
                                           [sem(f"p_ob_out{u}") for u in range(2)])
        vals_free, vals_out = sem("p_vals_free"), [sem(f"p_vals_out{u}") for u in range(2)]
        vals = sb("p_vals", [P, 2, 512])
        hi, lo = keep["hT_hi"], keep["hT_lo"]
        lb, oml = keep["lb"], keep["oml"]
        NG = len(GROUPS)
        NP = IV0 // 2
        iv_acc, iv_used, f_free = sem("p_iv_acc"), sem("p_iv_used"), sem("p_f_free")
        SECTIONS = [(Q0 // 2, 2, "q"), (F0 // 2, 4, "f"), (OG0 // 2, 2, "og"), (PU0 // 2, 2, "pu"), (GATE0 // 2, 8, "gate")]

        FUNCS = {"q": (ACT.Copy, -DESCALE * P ** -0.5), "f": (ACT.Sigmoid, DESCALE), "og": (ACT.Silu, DESCALE),
                 "pu": (ACT.Copy, DESCALE), "gate": (ACT.Sigmoid, DESCALE)}

        with nc.Block() as block:

            @block.sync
            def _(sp):
                with sp.Fori(0, NP) as i:
                    for u in range(2):
                        sp.wait_ge(wl_ready, i * 2 + u + 1)
                        sp.dma_start(raw[:, u], io["w_in"][i * 2 + u]).then_inc(raw_in[u], 16)
                sp.wait_ge(wl_ready, 2 * NP + 2)
                sp.dma_start(raw[:], io["w_in"][IV0:IV0 + 4].rearrange("b p k m -> p b k m")).then_inc(raw_in[0], 16)

            @block.gpsimd
            def _(pool):
                for first, pairs, kind in SECTIONS:
                    with pool.Fori(first, first + pairs) as i:
                        for u in range(2):
                            n = i * 2 + u
                            if kind == "f":
                                pool.wait_ge(f_ready, n - F0 + 1)
                            else:
                                pool.wait_ge(ob_ready, n + 1 if first < F0 // 2 else n + 1 - (OG0 - F0))
                            pool.dma_start(io["proj"][bass.ts(n, P), :], ob[:, u]).then_inc(ob_out[u], 16)
                pool.sem_inc(vals_free, 2)
                with pool.Fori(0, NT // 2) as i:
                    for u in range(2):
                        pool.wait_ge(iv_used, i * 2 + u + 3)
                        pool.dma_start(io["vals"][bass.ts(i * 2 + u, P), :], vals[:, u]).then_inc(vals_out[u], 16)
                    for u in range(2):
                        pool.wait_ge(vals_out[u], i * 16 + 16)
                        pool.sem_inc(vals_free, 1)
                for u in range(2):
                    pool.wait_ge(ob_out[u], 16 * NP)

            @block.scalar
            def _(act):
                def split(n, load, u, first=False):
                    act.wait_ge(raw_in[u], load * 16 + 16)
                    if not first:
                        act.wait_ge(acc_ready, n * NG)
                    nc.scalar.mul(wh[:, u], raw[:, u], W_SCALE).then_inc(wh_ready, 1)

                split(0, 0, 0, first=True)

                def pair(i, kind, at_start=False):
                    for u in range(2):
                        n = i * 2 + u
                        if kind == "gate" and u == 1:
                            with act.If(i < NP - 1):
                                split(n + 1, i + u, 1 - u)
                        else:
                            split(n + 1, i + u, 1 - u)
                        if kind == "f":
                            act.wait_ge(f_free, n - F0 + 1)
                        elif not at_start:
                            act.wait_ge(ob_out[u], i * 16)
                        for g, (t0, tn) in enumerate(GROUPS):
                            act.wait_ge(acc_ready, n * NG + NG + g + 1)
                            src = acc[:, g, 0:tn]
                            dst = sg if kind == "f" else ob
                            func, scale = FUNCS[kind]
                            nc.scalar.activation(dst[:, u, t0:t0 + tn], src, func, scale=scale).then_inc(acc_used, 1)
                        act.drain()
                        act.sem_inc(f_sig if kind == "f" else ob_ready, 1)

                for first, pairs, kind in SECTIONS:
                    if first == 0:
                        pair(0, kind, at_start=True)
                    with act.Fori(max(first, 1), first + pairs) as i:
                        pair(i, kind)
                act.wait_ge(raw_in[0], NP * 16 + 16)
                act.wait_ge(acc_ready, 2 * NP * NG + NG)
                nc.scalar.mul(wh[:], raw[:], W_SCALE).then_inc(wh_ready, 1)
                with act.Fori(0, NT // 2) as i:
                    for u in range(2):
                        act.wait_ge(iv_acc, i * 2 + u + 1)
                        act.wait_ge(vals_free, i * 2 + u + 1)
                        nc.scalar.activation(vals[:, u], acc[:, 6 + u], ACT.Copy, scale=DESCALE).then_inc(iv_used, 1)

            @block.vector
            def _(dve):
                dve.sem_inc(wl_ready, 2)
                dve.sem_inc(f_free, 2)

                def split(n, u):
                    dve.wait_ge(wh_ready, n + 1)
                    nc.vector.scalar_tensor_tensor(wl[:, u], raw[:, u], W_SCALE, wh[:, u], ALU.mult,
                                                   ALU.subtract).then_inc(wl_ready, 1)

                split(0, 0)
                for first, pairs, kind in SECTIONS:
                    with dve.Fori(first, first + pairs) as i:
                        for u in range(2):
                            n = i * 2 + u
                            if kind == "gate" and u == 1:
                                with dve.If(i < NP - 1):
                                    split(n + 1, 1 - u)
                            else:
                                split(n + 1, 1 - u)
                            if kind == "f":
                                dve.wait_ge(f_sig, n - F0 + 1)
                                dve.wait_ge(ob_out[u], i * 16)
                                nc.vector.tensor_scalar(ob[:, u], sg[:, u], oml[:, bass.ds(n - F0, 1)],
                                                        lb[:, bass.ds(n - F0, 1)], ALU.mult, ALU.add)
                                dve.drain()
                                dve.sem_inc(f_ready, 1)
                                dve.sem_inc(f_free, 1)
                dve.wait_ge(wh_ready, 2 * NP + 1)
                nc.vector.scalar_tensor_tensor(wl[:], raw[:], W_SCALE, wh[:], ALU.mult, ALU.subtract).then_inc(wl_ready, 1)

            @block.tensor
            def _(pe):
                pe.sem_inc(acc_ready, NG)
                pe.sem_inc(acc_used, NG)
                with pe.Fori(0, NP) as i:
                    for u in range(2):
                        pe.wait_ge(wl_ready, i * 2 + u + 3)
                        for g, (t0, n) in enumerate(GROUPS):
                            pe.wait_ge(acc_used, (i * 2 + u) * NG + g + 1)
                            for k in range(KD):
                                nc.tensor.matmul(acc[:, g, 0:n], wh[:, u, k], hi[:, k, t0:t0 + n], start=(k == 0), stop=False)
                                nc.tensor.matmul(acc[:, g, 0:n], wh[:, u, k], lo[:, k, t0:t0 + n], start=False, stop=False)
                                mm = nc.tensor.matmul(acc[:, g, 0:n], wl[:, u, k], hi[:, k, t0:t0 + n], start=False, stop=(k == KD - 1))
                            mm.then_inc(acc_ready, 1)
                pe.wait_ge(wl_ready, 2 * NP + 3)
                pe.sem_inc(iv_used, 2)
                with pe.Fori(0, NT // 2) as i:
                    for u in range(2):
                        pe.wait_ge(iv_used, i * 2 + u + 1)
                        for k in range(KD):
                            th, tl = hi[:, k, bass.ts(i * 2 + u, P)], lo[:, k, bass.ts(i * 2 + u, P)]
                            nc.tensor.matmul(acc[:, 6 + u], th, wh[:, :, k], start=(k == 0), stop=False)
                            nc.tensor.matmul(acc[:, 6 + u], tl, wh[:, :, k], start=False, stop=False)
                            mm = nc.tensor.matmul(acc[:, 6 + u], th, wl[:, :, k], start=False, stop=(k == KD - 1))
                        mm.then_inc(iv_acc, 1)



def stage_scan(nc, io, keep):
    with ExitStack() as ctx:
        def sb(n, s, d=F32):
            return [ctx.enter_context(nc.sbuf_tensor(f"{n}{r}", s, d)) for r in range(2)]

        def sem(n):
            return [nc.alloc_semaphore(f"s_{n}{r}") for r in range(2)]

        W = HEADS * P
        f_in, q_in, v_in = sb("s_f", [P, 2, W]), sb("s_q", [P, 2, W]), sb("s_v", [P, 2, W])
        g, cum, ex = sb("s_g", [P, W]), sb("s_cum", [P, W]), sb("s_ex", [P, W])
        e1, e2 = sb("s_e1", [P, W]), sb("s_e2", [P, W])
        qt, kt, qh, kh = sb("s_qt", [P, W]), sb("s_kt", [P, W]), sb("s_qh", [P, W]), sb("s_kh", [P, W])
        khT, scm = sb("s_khT", [P, W]), sb("s_scm", [P, W])
        lm, dec = sb("s_lm", [P, 16]), sb("s_dec", [P, 3, 16])
        S = sb("s_S", [P, 2 * CPT, W])
        fin, st0 = sb("s_fin", [P, W]), sb("s_st0", [P, W])
        mask, reset = sb("s_mask", [P, W], U32), sb("s_reset", [P, W])
        ident = ctx.enter_context(nc.sbuf_tensor("s_ident", [P, P], F32))
        ps = lambda n: [ctx.enter_context(nc.psum_tensor(f"{n}{r}", [P, W], F32)) for r in range(2)]
        sc_ps, tr_ps, u_ps, o_ps = ps("s_scp"), ps("s_trp"), ps("s_up"), ps("s_op")
        consts = nc.alloc_semaphore("s_consts")
        tick = nc.alloc_semaphore("s_tick")
        tick_sp = nc.alloc_semaphore("s_tick_sp")
        ins_in = [[nc.alloc_semaphore(f"s_in{r}{u}") for u in range(2)] for r in range(2)]
        g_ready, cum_ready, e_ready, qk_ready, kh_ready = sem("g"), sem("cum"), sem("e"), sem("qk"), sem("kh")
        sc_ready, tr_ready, m_ready, khT_ready = sem("sc"), sem("tr"), sem("m"), sem("khT")
        u_ready, st_ready, o_ready, oc_ready = sem("u"), sem("st"), sem("o"), sem("oc")
        fin_ready, fin_out = sem("fin"), sem("fin_out")
        oT = keep["oT"]
        MID, LAST = (15, 16), (31, 0)
        order = (range(CPT), range(CPT - 1, -1, -1))
        at = lambda t, pos: t[:].rearrange("p (n c) -> p n c", c=CHUNK)[:, :, pos]
        per_chunk = lambda t: t[:].rearrange("p (n c) -> p n c", c=CHUNK)
        wide = lambda t: t.unsqueeze(2).to_broadcast([P, 16, CHUNK])

        def tile_of(r, j, u, latent):
            if r == 0:
                return j * 2 + u
            return 19 - u - j * 2 if latent else 1 - u

        def steps(eng, body, between=None):
            for u in range(2):
                body(0, u, False)
            if between:
                between()
            with eng.Fori(1, NT // 2) as j:
                for u in range(2):
                    body(j, u, True)

        with nc.Block() as block:

            @block.sync
            def _(sp):
                for dst, src in ((mask[0], "mask_f"), (mask[1], "mask_b"), (reset[0], "reset_f"), (reset[1], "reset_b"),
                                 (ident, "ident"), (st0[0], "state_f"), (st0[1], "state_b")):
                    sp.dma_start(dst[:], io[src]).then_inc(consts, 16)

                def body(j, u, latent):
                    for r in range(2):
                        t = tile_of(r, j, u, latent)
                        sp.wait_ge(qk_ready[r], j * 2 + u + 1)
                        sp.wait_ge(o_ready[r], j * 2 + u + 1)
                        sp.sem_inc(tick_sp, 1)
                        for dst, row in ((q_in[r], 0), (f_in[r], W * (1 + r))):
                            sp.dma_start(dst[:, u].rearrange("p (h t) -> p h t", h=HEADS),
                                         io["proj"][row:row + W, bass.ts(t, P)].rearrange("(h p) t -> p h t", p=P)
                                         ).then_inc(ins_in[r][u], 16)
                        sp.dma_start(v_in[r][:, u], io["vals"][bass.ts(t, P), :]).then_inc(ins_in[r][u], 16)

                def save():
                    for r in range(2):
                        sp.wait_ge(fin_ready[r], 1)
                        sp.dma_start(io["new_state"][r].rearrange("h k v -> k h v"),
                                     fin[r][:].rearrange("p (h v) -> p h v", h=HEADS)).then_inc(fin_out[r], 16)
                steps(sp, body)
                save()
                for r in range(2):
                    sp.wait_ge(fin_out[r], 16)

            @block.scalar
            def _(act):
                for r in range(2):
                    act.sem_inc(e_ready[r], 1)
                    act.sem_inc(khT_ready[r], 1)
                    act.sem_inc(oc_ready[r], 1)

                def body(j, u, latent):
                    s = j * 2 + u
                    for r in range(2):
                        act.wait_ge(ins_in[r][u], j * 48 + 48)
                        act.wait_ge(cum_ready[r], s + 1)
                        nc.scalar.activation(g[r][:], f_in[r][:, u], ACT.Ln).then_inc(g_ready[r], 1)
                    for r in range(2):
                        act.wait_ge(cum_ready[r], s + 2)
                        act.wait_ge(qk_ready[r], s + 2)
                        act.wait_ge(kh_ready[r], s + 1)
                        act.wait_ge(st_ready[r], s * CPT + 1)
                        nc.scalar.activation(e1[r][:], ex[r][:], ACT.Exp)
                        nc.scalar.activation(e2[r][:], ex[r][:], ACT.Exp, scale=-1.0)
                        nc.scalar.activation(dec[r][:, 0], at(cum[r], MID[r]), ACT.Exp)
                        nc.scalar.activation(dec[r][:, 1], lm[r][:], ACT.Exp)
                        nc.scalar.activation(dec[r][:, 2], at(cum[r], LAST[r]), ACT.Exp).then_inc(e_ready[r], 1)
                    for r in range(2):
                        act.wait_ge(tr_ready[r], s + 2)
                        act.wait_ge(u_ready[r], s * CPT + 1)
                        nc.scalar.copy(khT[r][:], tr_ps[r][:]).then_inc(khT_ready[r], 1)
                    for r in range(2):
                        act.wait_ge(o_ready[r], s + 3)
                        nc.scalar.copy(oT[r][:, :, bass.ts(tile_of(r, j, u, latent), P)],
                                       o_ps[r][:].rearrange("p (h t) -> p h t", h=HEADS)).then_inc(oc_ready[r], 1)
                steps(act, body)

            @block.gpsimd
            def _(pool):
                for r in range(2):
                    pool.sem_inc(kh_ready[r], 1)

                def body(j, u, latent):
                    s = j * 2 + u
                    for r in range(2):
                        pool.wait_ge(qk_ready[r], s + 3)
                        pool.wait_ge(o_ready[r], s + 2)
                        nc.gpsimd.tensor_tensor(per_chunk(kh[r]), per_chunk(kt[r]), wide(dec[r][:, 1]), ALU.mult)
                        nc.gpsimd.tensor_tensor(per_chunk(qh[r]), per_chunk(qt[r]), wide(dec[r][:, 0]), ALU.mult
                                                ).then_inc(kh_ready[r], 1)
                steps(pool, body)

            @block.vector
            def _(dve):
                dve.wait_ge(consts, 7 * 16)
                for r in range(2):
                    nc.vector.memset(scm[r][:], 0.0)
                    nc.vector.memset(S[r][:, 0], 0.0)
                    dve.sem_inc(cum_ready[r], 1)
                    dve.sem_inc(qk_ready[r], 2)
                    dve.sem_inc(m_ready[r], 1)
                    dve.sem_inc(st_ready[r], 1)
                dve.drain()

                def body(j, u, latent):
                    s = j * 2 + u
                    rev = lambda r, t: t[:] if r == 0 else t[:, ::-1]
                    for r in range(2):
                        dve.wait_ge(g_ready[r], s + 1)
                        dve.wait_ge(e_ready[r], s + 1)
                        nc.vector.tensor_tensor_scan(rev(r, cum[r]), rev(r, reset[r]), rev(r, g[r]), 0.0, ALU.mult, ALU.add)
                    dve.drain()
                    for r in range(2):
                        nc.vector.tensor_tensor(per_chunk(ex[r]), per_chunk(cum[r]), wide(at(cum[r], MID[r])), ALU.subtract)
                        nc.vector.tensor_tensor(lm[r][:], at(cum[r], LAST[r]), at(cum[r], MID[r]), ALU.subtract)
                    dve.drain()
                    for r in range(2):
                        nc.vector.tensor_scalar(ex[r][:], ex[r][:], 80.0, -80.0, ALU.min, ALU.max).then_inc(cum_ready[r], 1)
                    for r in range(2):
                        dve.wait_ge(e_ready[r], s + 2)
                        dve.wait_ge(kh_ready[r], s + 1)
                        dve.wait_ge(sc_ready[r], s + 1)
                        nc.vector.tensor_tensor(qt[r][:], q_in[r][:, u], e1[r][:], ALU.mult)
                        nc.vector.scalar_tensor_tensor(kt[r][:], f_in[r][:, u], 1.0, e2[r][:], ALU.subtract, ALU.mult
                                                       ).then_inc(qk_ready[r], 1)
                    for r in range(2):
                        dve.wait_ge(sc_ready[r], s + 2)
                        dve.wait_ge(o_ready[r], s + 2)
                        dve.sem_inc(tick, 1)
                        nc.vector.copy_predicated(scm[r][:], mask[r][:], sc_ps[r][:]).then_inc(m_ready[r], 1)
                    for c in range(CPT):
                        for r in range(2):
                            dve.wait_ge(u_ready[r], s * CPT + c + 2)
                            old, new, ch = CPT * u + c, (CPT * u + c + 1) % (2 * CPT), order[r][c]
                            for h in range(HEADS):
                                hs = slice(h * P, (h + 1) * P)
                                ins = nc.vector.scalar_tensor_tensor(S[r][:, new, hs], S[r][:, old, hs],
                                                                     dec[r][:, 2, h * CPT + ch:h * CPT + ch + 1],
                                                                     u_ps[r][:, hs], ALU.mult, ALU.add)
                            ins.then_inc(st_ready[r], 1)
                        dve.drain()

                def latent_start():
                    for r in range(2):
                        nc.vector.tensor_scalar(fin[r][:], S[r][:, 0], -1.0, None, ALU.mult).then_inc(fin_ready[r], 1)
                    dve.drain()
                    for r in range(2):
                        nc.vector.tensor_scalar(S[r][:, 0], st0[r][:], -1.0, None, ALU.mult)
                    dve.drain()
                steps(dve, body, latent_start)

            @block.tensor
            def _(pe):
                for r in range(2):
                    pe.sem_inc(sc_ready[r], 1)
                    pe.sem_inc(tr_ready[r], 1)
                    pe.sem_inc(u_ready[r], 1)
                    pe.sem_inc(o_ready[r], 2)
                pe.wait_ge(consts, 7 * 16)

                def body(j, u, latent):
                    s = j * 2 + u
                    for r in range(2):
                        pe.wait_ge(qk_ready[r], s + 3)
                        pe.wait_ge(m_ready[r], s + 1)
                        for h in range(HEADS):
                            hs = slice(h * P, (h + 1) * P)
                            mm = nc.tensor.matmul(sc_ps[r][:, hs], kt[r][:, hs], qt[r][:, hs], start=True, stop=True)
                        mm.then_inc(sc_ready[r], 1)
                    for r in range(2):
                        pe.wait_ge(kh_ready[r], s + 2)
                        pe.wait_ge(khT_ready[r], s + 1)
                        for h in range(HEADS):
                            hs = slice(h * P, (h + 1) * P)
                            mm = nc.tensor.transpose(tr_ps[r][:, hs], kh[r][:, hs], ident[:])
                        mm.then_inc(tr_ready[r], 1)
                    for c in range(CPT):
                        for r in range(2):
                            ch = order[r][c]
                            rows = slice(ch * CHUNK, (ch + 1) * CHUNK)
                            if c == 0:
                                pe.wait_ge(khT_ready[r], s + 2)
                            pe.wait_ge(st_ready[r], s * CPT + c + 1)
                            for h in range(HEADS):
                                hs = slice(h * P, (h + 1) * P)
                                mm = nc.tensor.matmul(u_ps[r][:, hs], khT[r][rows, hs], v_in[r][rows, u, hs], start=True, stop=True)
                            mm.then_inc(u_ready[r], 1)
                    for r in range(2):
                        pe.wait_ge(m_ready[r], s + 2)
                        pe.wait_ge(st_ready[r], s * CPT + CPT)
                        pe.wait_ge(oc_ready[r], s + 1)
                        for h in range(HEADS):
                            hs = slice(h * P, (h + 1) * P)
                            nc.tensor.matmul(o_ps[r][:, hs], v_in[r][:, u, hs], scm[r][:, hs], start=True, stop=False)
                            for c in range(CPT):
                                cs = slice(h * P + order[r][c] * CHUNK, h * P + (order[r][c] + 1) * CHUNK)
                                mm = nc.tensor.matmul(o_ps[r][:, cs], S[r][:, CPT * u + c, hs], qh[r][:, cs],
                                                      start=False, stop=(c == CPT - 1))
                        mm.then_inc(o_ready[r], 1)
                steps(pe, body)


def stage_hgrn_out(nc, io, keep):
    W = HEADS * P
    with ExitStack() as ctx:
        sb = lambda n, s, d=F32: ctx.enter_context(nc.sbuf_tensor(n, s, d))
        sem = nc.alloc_semaphore
        og = sb("h_og", [P, 2, HEADS, P])
        o, sq, y = sb("h_o", [P, 2, HEADS, P]), sb("h_sq", [P, 2, W]), sb("h_y", [P, 2, HEADS, P])
        ms, rstd = sb("h_ms", [P, 2, W]), sb("h_rstd", [P, 2, W])
        eps, ones, ng = sb("h_eps", [P, 1]), sb("h_ones", [P, P]), sb("h_ng", [P, 1])
        acc = ctx.enter_context(nc.psum_tensor("h_acc", [P, 2, W], F32))
        og_in = [sem(f"h_og_in{u}") for u in range(2)]
        ng_in, o_ready, sq_ready, ms_ready = sem("h_ng_in"), sem("h_os"), sem("h_sqs"), sem("h_mss")
        sum_ready, y_ready, hi_ready, ones_ready = sem("h_sum"), sem("h_yr"), sem("h_hi"), sem("h_ones_ready")
        lo_ready, ya_out = sem("h_lo"), [sem(f"h_out{u}") for u in range(2)]
        tick_sp = sem("h_tick_sp")
        hl = sb("h_hl", [P, 2, 2, HEADS, P], F16)
        oT = keep["oT"]
        flat = lambda t, u: t[:, u].rearrange("p h t -> p (h t)")

        with nc.Block() as block:

            @block.sync
            def _(sp):
                sp.dma_start(ng[:], io["hgrn_norm_c"]).then_inc(ng_in, 16)
                for u in range(2):
                    sp.sem_inc(ya_out[u], 16)
                with sp.Fori(0, NT // 2) as i:
                    for u in range(2):
                        sp.wait_ge(y_ready, i * 2 + u + 1)
                        sp.dma_start(og[:, u], io["proj"][OG0 * P:(OG0 + 4) * P, bass.ts(i * 2 + u, P)].rearrange(
                            "(h p) t -> p h t", p=P)).then_inc(og_in[u], 16)
                    for u in range(2):
                        sp.wait_ge(lo_ready, i * 2 + u + 1)
                        sp.sem_inc(tick_sp, 1)
                        sp.dma_start(io["yab"][:, 0:8, bass.ts(i * 2 + u, P)],
                                     hl[:, u].rearrange("p q h t -> p (q h) t")).then_inc(ya_out[u], 16)
                for u in range(2):
                    sp.wait_ge(ya_out[u], 16 * (NT // 2) + 16)

            @block.scalar
            def _(act):
                act.sem_inc(sq_ready, 2)
                act.sem_inc(hi_ready, 2)
                act.sem_inc(ms_ready, 2)
                act.wait_ge(ones_ready, 1)
                with act.Fori(0, NT // 2) as i:
                    for u in range(2):
                        act.wait_ge(o_ready, i * 2 + u + 3)
                        act.wait_ge(sum_ready, i * 2 + u + 1)
                        nc.scalar.activation(sq[:, u], flat(o, u), ACT.Square).then_inc(sq_ready, 1)
                    for u in range(2):
                        act.wait_ge(sum_ready, i * 2 + u + 3)
                        act.wait_ge(y_ready, i * 2 + u + 1)
                        nc.scalar.activation(ms[:, u], acc[:, u], ACT.Sqrt, bias=eps[:], scale=1.0 / P).then_inc(ms_ready, 1)
                    for u in range(2):
                        act.wait_ge(y_ready, i * 2 + u + 3)
                        act.wait_ge(ya_out[u], i * 16 + 16)
                        nc.scalar.copy(hl[:, u, 0], y[:, u]).then_inc(hi_ready, 1)

            @block.gpsimd
            def _(pool):
                nc.gpsimd.memset(eps[:], EPS)
                nc.gpsimd.memset(ones[:], 1.0)
                pool.drain()
                pool.sem_inc(ones_ready, 1)

            @block.vector
            def _(dve):
                dve.sem_inc(o_ready, 2)
                dve.sem_inc(y_ready, 2)
                dve.wait_ge(ng_in, 16)
                nc.vector.tensor_scalar(ng[:], ng[:], X_SCALE, None, ALU.mult)
                dve.drain()
                with dve.Fori(0, NT // 2) as i:
                    for u in range(2):
                        ts = bass.ts(i * 2 + u, P)
                        nc.vector.tensor_tensor(o[:, u], oT[0][:, :, ts], oT[1][:, :, ts], ALU.add).then_inc(o_ready, 1)
                    for u in range(2):
                        dve.wait_ge(ms_ready, i * 2 + u + 3)
                        nc.vector.reciprocal(rstd[:, u], ms[:, u])
                    dve.drain()
                    for u in range(2):
                        nc.vector.scalar_tensor_tensor(flat(y, u), flat(o, u), ng[:], rstd[:, u], ALU.mult, ALU.mult)
                    dve.drain()
                    for u in range(2):
                        dve.wait_ge(og_in[u], i * 16 + 16)
                        nc.vector.tensor_tensor(y[:, u], y[:, u], og[:, u], ALU.mult).then_inc(y_ready, 1)
                    for u in range(2):
                        dve.wait_ge(hi_ready, i * 2 + u + 3)
                        nc.vector.tensor_tensor(hl[:, u, 1], y[:, u], hl[:, u, 0], ALU.subtract).then_inc(lo_ready, 1)

            @block.tensor
            def _(pe):
                pe.sem_inc(sum_ready, 2)
                pe.wait_ge(ones_ready, 1)
                with pe.Fori(0, NT // 2) as i:
                    for u in range(2):
                        pe.wait_ge(sq_ready, i * 2 + u + 3)
                        pe.wait_ge(ms_ready, i * 2 + u + 1)
                        nc.tensor.matmul(acc[:, u], ones[:], sq[:, u], start=True, stop=True).then_inc(sum_ready, 1)



def stage_pooling(nc, io, keep):
    PAD = max(WINDOWS) // 2
    CW, RH = GRID_W + 2 * PAD, GRID_H + 2 * PAD
    with ExitStack() as ctx:
        sb = lambda n, s, d=F32: ctx.enter_context(nc.sbuf_tensor(n, s, d))
        sem = nc.alloc_semaphore
        NG = len(WINDOWS)
        uT = sb("o_u", [P, 2, T])
        cpad, rpad = sb("o_cpad", [P, GRID_H, CW]), sb("o_rpad", [P, RH, GRID_W])
        spad = sb("o_spad", [P, CTX + 2 * PAD])
        tmp = [sb(f"o_tmp{n}", [P, RH * GRID_W]) for n in range(2)]
        d = sb("o_d", [P, 2, T])
        y = sb("o_y", [P, T])
        hl = sb("o_hl", [P, 2, T], F16)
        inv = sb("o_inv", [P, NG, GRID_H + GRID_W + CTX])
        wp, pscale = sb("o_wp", [P, NG, P]), sb("o_pscale", [P, NG])
        acc = ctx.enter_context(nc.psum_tensor("o_acc", [P, len(GROUPS), 512], F32))
        consts, u_in, y_out = sem("o_consts"), [sem(f"o_in{u}") for u in range(2)], sem("o_out")
        d_ready, acc_ready, y_ready, hi_ready, lo_ready = sem("o_dr"), sem("o_acc_r"), sem("o_yr"), sem("o_hi"), sem("o_lo")

        with nc.Block() as block:

            @block.sync
            def _(sp):
                sp.dma_start(inv[:], io["pool_inv"].partition_broadcast(P)).then_inc(consts, 16)
                sp.dma_start(wp[:], io["w_pool_l"]).then_inc(consts, 16)
                sp.dma_start(pscale[:], io["pool_scale_c"]).then_inc(consts, 16)
                for g in range(NG):
                    if g >= 2:
                        sp.wait_ge(d_ready, g - 1)
                    sp.dma_start(uT[:, g % 2], io["proj"][(PU0 + g) * P:(PU0 + g + 1) * P, :]).then_inc(u_in[g % 2], 16)
                for g in range(NG):
                    sp.wait_ge(lo_ready, g + 1)
                    for q in range(2):
                        sp.dma_start(io["yab"][:, 8 + q * HEADS + g, :], hl[:, q]).then_inc(y_out, 16)
                sp.wait_ge(y_out, NG * 32)

            @block.vector
            def _(dve):
                for b in (cpad, rpad, spad):
                    nc.vector.memset(b[:], 0.0)
                dve.wait_ge(consts, 48)
                nc.vector.tensor_scalar(pscale[:], pscale[:], X_SCALE, None, ALU.mult)
                dve.drain()

                for g, w in enumerate(WINDOWS):
                    b = g % 2
                    dve.wait_ge(u_in[b], 16 * (g // 2) + 16)
                    lat = uT[:, b, CTX:].rearrange("p (r c) -> p r c", c=GRID_W)
                    nc.vector.tensor_copy(cpad[:, :, PAD:PAD + GRID_W], lat)
                    nc.vector.tensor_copy(spad[:, PAD:PAD + CTX], uT[:, b, 0:CTX])
                    dve.drain()
                    if g >= 2:
                        dve.wait_ge(acc_ready, g - 1)
                    s0 = PAD - w // 2
                    dl = d[:, b, CTX:].rearrange("p (r c) -> p r c", c=GRID_W)
                    src, step, flip = cpad[:], 1, 0
                    while 2 * step < w:
                        m = CW - 2 * step + 1
                        dst = tmp[flip][:, 0:GRID_H * m].rearrange("p (r c) -> p r c", c=m)
                        nc.vector.tensor_tensor(dst, src[:, :, 0:m], src[:, :, step:step + m], ALU.add)
                        dve.drain()
                        src, step, flip = dst, 2 * step, 1 - flip
                    nc.vector.tensor_tensor(rpad[:, PAD:PAD + GRID_H, :], src[:, :, s0:s0 + GRID_W],
                                            src[:, :, s0 + step:s0 + step + GRID_W], ALU.add)
                    dve.drain()
                    src, step, flip = rpad[:], 1, 0
                    while 2 * step < w:
                        m = RH - 2 * step + 1
                        dst = tmp[flip][:, 0:m * GRID_W].rearrange("p (r c) -> p r c", c=GRID_W)
                        nc.vector.tensor_tensor(dst, src[:, 0:m, :], src[:, step:step + m, :], ALU.add)
                        dve.drain()
                        src, step, flip = dst, 2 * step, 1 - flip
                    nc.vector.tensor_tensor(dl, src[:, s0:s0 + GRID_H, :], src[:, s0 + step:s0 + step + GRID_H, :], ALU.add)
                    src, step, flip = spad[:], 1, 0
                    dve.drain()
                    while 2 * step < w:
                        m = CTX + 2 * PAD - 2 * step + 1
                        dst = tmp[flip][:, 0:m]
                        nc.vector.tensor_tensor(dst, src[:, 0:m], src[:, step:step + m], ALU.add)
                        dve.drain()
                        src, step, flip = dst, 2 * step, 1 - flip
                    nc.vector.tensor_tensor(d[:, b, 0:CTX], src[:, s0:s0 + CTX], src[:, s0 + step:s0 + step + CTX], ALU.add)
                    dve.drain()
                    nc.vector.tensor_tensor(dl, dl, inv[:, g, 0:GRID_H].unsqueeze(2).to_broadcast([P, GRID_H, GRID_W]), ALU.mult)
                    nc.vector.tensor_tensor(d[:, b, 0:CTX], d[:, b, 0:CTX], inv[:, g, GRID_H + GRID_W:], ALU.mult)
                    dve.drain()
                    nc.vector.tensor_tensor(dl, dl, inv[:, g, GRID_H:GRID_H + GRID_W].unsqueeze(1).to_broadcast([P, GRID_H, GRID_W]), ALU.mult)
                    dve.drain()
                    nc.vector.tensor_tensor(d[:, b], d[:, b], uT[:, b], ALU.subtract).then_inc(d_ready, 1)
                    dve.wait_ge(acc_ready, g + 1)
                    for n, (t0, tn) in enumerate(GROUPS):
                        nc.vector.tensor_scalar(y[:, t0:t0 + tn], acc[:, n, 0:tn], pscale[:, g:g + 1], None, ALU.mult)
                    dve.drain()
                    dve.sem_inc(y_ready, 1)
                    dve.wait_ge(hi_ready, g + 1)
                    nc.vector.tensor_tensor(hl[:, 1], y[:], hl[:, 0], ALU.subtract).then_inc(lo_ready, 1)

            @block.scalar
            def _(act):
                for g in range(NG):
                    act.wait_ge(y_ready, g + 1)
                    if g:
                        act.wait_ge(y_out, 32 * g)
                    nc.scalar.copy(hl[:, 0], y[:]).then_inc(hi_ready, 1)

            @block.tensor
            def _(pe):
                pe.wait_ge(consts, 48)
                for g in range(NG):
                    pe.wait_ge(d_ready, g + 1)
                    if g:
                        pe.wait_ge(y_ready, g)
                    for n, (t0, tn) in enumerate(GROUPS):
                        mm = nc.tensor.matmul(acc[:, n, 0:tn], wp[:, g], d[:, g % 2, t0:t0 + tn], start=True, stop=True)
                    mm.then_inc(acc_ready, 1)


def stage_merge(nc, io, keep):
    N = 2 * P
    with ExitStack() as ctx:
        sb = lambda n, s, d=F32: ctx.enter_context(nc.sbuf_tensor(n, s, d))
        sem = nc.alloc_semaphore
        raw = sb("g_raw", [P, 2, D])
        wh, wl = sb("g_wh", [P, 16, D], F16), sb("g_wl", [P, 16, D], F16)
        yin = sb("g_yin", [P, 2, 16, N], F16)
        sg = sb("g_sg", [P, 16, N])
        t1, t2 = sb("g_t1", [P, 2, N]), sb("g_t2", [P, 2, N])
        mh, ml = sb("g_mh", [P, KD, N], F16), sb("g_ml", [P, KD, N], F16)
        rows = sb("g_rows", [P, 3, D])
        x = sb("g_x", [P, 2, 2, D])
        h2 = sb("g_h2", [P, 2, D])
        hl = sb("g_hl", [P, 2, 2, D], F16)
        junk = sb("g_junk", [P, D], F16)
        hT = sb("g_hT", [P, KD, P])
        wr, br, iota, ident = sb("g_wr", [P, KD, E]), sb("g_br", [P, E]), sb("g_iota", [P, E]), sb("g_ident", [P, P])
        ss, ms, rstd, mhalf = sb("g_ss", [P, 2]), sb("g_ms", [P, 2]), sb("g_rstd", [P, 2]), sb("g_mhalf", [P, 1])
        lg, mv, ixu, ixf = sb("g_lg", [P, E]), sb("g_mv", [P, 8]), sb("g_ixu", [P, 8], U32), sb("g_ixf", [P, TOPK])
        nm, ex, se, rs, wk = sb("g_nm", [P, 1]), sb("g_ex", [P, TOPK]), sb("g_se", [P, 1]), sb("g_rs", [P, 1]), sb("g_wk", [P, TOPK])
        oh, ohw = sb("g_oh", [P, TOPK, E]), sb("g_ohw", [P, TOPK, E])
        pa = [ctx.enter_context(nc.psum_tensor(f"g_pa{u}", [P, 2, N], F32)) for u in range(2)]
        pb = [ctx.enter_context(nc.psum_tensor(f"g_pb{u}", [P, 2, N], F32)) for u in range(2)]
        po = ctx.enter_context(nc.psum_tensor("g_po", [P, D], F32))
        pt = ctx.enter_context(nc.psum_tensor("g_pt", [P, D], F32))
        raw_in, consts = [sem(f"g_raw_in{u}") for u in range(2)], sem("g_consts")
        wh_ready, wl_ready, rows_in, rows2_in = sem("g_whr"), sem("g_wlr"), sem("g_rows_in"), sem("g_rows2_in")
        y_in, sg_in, x_in = [sem(f"g_y_in{u}") for u in range(2)], sem("g_sg_in"), [sem(f"g_x_in{u}") for u in range(2)]
        br_ready, br_used, m_ready, mh_ready = sem("g_br_r"), sem("g_br_u"), sem("g_m_r"), sem("g_mh_r")
        ml_ready, po_ready, po_used, x1_ready = sem("g_ml_r"), sem("g_po_r"), sem("g_po_u"), sem("g_x1_r")
        ss_ready, rstd_ready, h2_ready, hi_ready, hl_ready = (sem("g_ss_r"), sem("g_rstd_r"), sem("g_h2_r"),
                                                              sem("g_hi_r"), sem("g_hl_r"))
        tr_ready, hT_ready, lg_ready, lg_used = sem("g_tr_r"), sem("g_hT_r"), sem("g_lg_r"), sem("g_lg_u")
        top_ready, ex_done, st_out, st_free = sem("g_top_r"), sem("g_ex_d"), sem("g_st_out"), sem("g_st_free")
        tick, tick_p, tick_sp = sem("g_tick"), sem("g_tick_p"), sem("g_tick_sp")
        M_all, Wd_all, ix_all, w_all = keep["M_all"], keep["Wd_all"], keep["ix_all"], keep["w_all"]
        mrows = io["mod_rows"].rearrange("(v q k) p -> v q (k p)", v=2, q=4)
        NGR = T // N
        LAST_B = (NGR - 1) % 2

        def groups(eng, body, between=None):
            body(0, 0, None)
            if between:
                between()
            with eng.Fori(0, (NGR - 1) // 2) as i:
                for u in range(2):
                    body(i * 2 + u + 1, 1 - u, i)

        def x_count(i, b):
            return i * 16 + 16 * (2 - b)

        with nc.Block() as block:

            @block.sync
            def _(sp):
                for dst, src in ((wr, "w_router_l"), (ident, "ident")):
                    sp.dma_start(dst[:], io[src]).then_inc(consts, 16)
                sp.dma_start(br[:], io["b_router"].partition_broadcast(P)).then_inc(consts, 16)
                sp.dma_start(iota[:], io["iota"][0:E].partition_broadcast(P)).then_inc(consts, 16)
                for q in range(3):
                    sp.dma_start(rows[:, q], mrows[0, q].partition_broadcast(P)).then_inc(rows_in, 16)
                with sp.Fori(0, 8) as i:
                    for u in range(2):
                        sp.wait_ge(wl_ready, i * 2 + u + 1)
                        sp.dma_start(raw[:, u], io["w_merge"][bass.ts(i * 2 + u, P), :]).then_inc(raw_in[u], 16)

                def body(n, b, i):
                    sp.wait_ge(ml_ready, n * 4 + 1)
                    for dst, src, s in ((yin[:, b], io["yab"][:, :, bass.ts(n, N)], y_in[b]),
                                        (sg[:], io["proj"][GATE0 * P:(GATE0 + 16) * P, bass.ts(n, N)].rearrange("(m p) t -> p m t", p=P), sg_in)):
                        sp.dma_start(dst, src).then_inc(s, 16)
                    sp.wait_ge(st_free, n * 2 + 1)
                    sp.sem_inc(tick_sp, 1)
                    sp.dma_start(x[:, b], io["x"][bass.ts(n, N), :].rearrange("(c p) d -> p c d", p=P)).then_inc(x_in[b], 16)

                groups(sp, body)

            @block.scalar
            def _(act):
                act.sem_inc(hT_ready, 1)
                with act.Fori(0, 8) as i:
                    for u in range(2):
                        act.wait_ge(raw_in[u], i * 16 + 16)
                        nc.scalar.mul(wh[:, i * 2 + u], raw[:, u], W_SCALE).then_inc(wh_ready, 1)
                act.wait_ge(consts, 64)

                def hT_copy(t):
                    act.wait_ge(tr_ready, t + 3)
                    nc.scalar.copy(hT[:].rearrange("p k t -> p (k t)"), pt[:]).then_inc(hT_ready, 1)

                def exp(t):
                    act.wait_ge(top_ready, t + 1)
                    nc.scalar.activation(ex[:], mv[:, 0:TOPK], ACT.Exp, bias=nm[:], accum_out=se[:])
                    act.drain()
                    act.sem_inc(ex_done, 1)

                def merged(n, m):
                    act.wait_ge(m_ready, n * 4 + m + 1)
                    if m == 0:
                        act.wait_ge(po_ready, n * 2 + 1)
                    nc.scalar.copy(mh[:, 2 * m:2 * m + 2], t1[:]).then_inc(mh_ready, 1)

                def square(t, b, c):
                    act.wait_ge(x1_ready, t + 1)
                    act.wait_ge(rstd_ready, t + 1)
                    nc.scalar.activation(junk[:], x[:, b, c], ACT.Square, accum_out=ss[:, c:c + 1]).then_inc(ss_ready, 1)
                    act.drain()

                def high(t, c):
                    act.wait_ge(h2_ready, t + 3)
                    act.wait_ge(st_free, t + 2)
                    nc.scalar.copy(hl[:, c, 0], h2[:, c]).then_inc(hi_ready, 1)

                def body(n, b, i):
                    t = n * 2
                    if i is not None:
                        square(t - 1, 1 - b, 1)
                        hT_copy(t - 2)
                        high(t - 1, 1)
                    merged(n, 0)
                    if i is not None:
                        exp(t - 2)
                    merged(n, 1)
                    if i is not None:
                        hT_copy(t - 1)
                    merged(n, 2)
                    if i is not None:
                        exp(t - 1)
                    merged(n, 3)
                    square(t, b, 0)
                    high(t, 0)
                act.sem_inc(ex_done, 1)
                groups(act, body)
                square(NT - 1, LAST_B, 1)
                hT_copy(NT - 2)
                high(NT - 1, 1)
                exp(NT - 2)
                hT_copy(NT - 1)
                exp(NT - 1)

            @block.gpsimd
            def _(pool):
                nc.gpsimd.memset(mhalf[:], -0.5)
                pool.drain()
                pool.sem_inc(rstd_ready, 2)
                pool.sem_inc(st_free, 3)

                def stored(t):
                    pool.wait_ge(st_out, t * 32 + 32)
                    pool.sem_inc(st_free, 1)

                def body(n, b, i):
                    for c in range(2):
                        t = n * 2 + c
                        pool.wait_ge(ss_ready, t + 1)
                        pool.wait_ge(h2_ready, t + 1)
                        pool.sem_inc(tick_p, 1)
                        nc.gpsimd.tensor_scalar(ms[:, c:c + 1], ss[:, c:c + 1], 1.0 / D, EPS, ALU.mult, ALU.add)
                        pool.drain()
                        nc.gpsimd.tensor_tensor(rstd[:, c:c + 1], ms[:, c:c + 1], mhalf[:], ALU.pow).then_inc(rstd_ready, 1)
                        if i is not None or c:
                            stored(t - 1)
                        pool.wait_ge(hl_ready, t + 1)
                        pool.dma_start(io["x1"][bass.ts(t, P), :], x[:, b, c]).then_inc(st_out, 16)
                        pool.dma_start(io["h2"][bass.ts(t, P), :], hl[:, c].rearrange("p q d -> p (q d)")).then_inc(st_out, 16)

                def latent_rows():
                    pool.wait_ge(h2_ready, 2 + 2)
                    for q in range(3):
                        pool.dma_start(rows[:, q], mrows[1, q].partition_broadcast(P)).then_inc(rows2_in, 16)
                groups(pool, body, latent_rows)
                stored(NT - 1)

            @block.vector
            def _(dve):
                dve.sem_inc(wl_ready, 2)
                dve.sem_inc(ml_ready, 1)
                dve.sem_inc(h2_ready, 2)
                dve.sem_inc(br_used, 2)
                dve.sem_inc(po_used, 1)
                dve.sem_inc(lg_used, 1)
                with dve.Fori(0, 8) as i:
                    for u in range(2):
                        dve.wait_ge(wh_ready, i * 2 + u + 1)
                        nc.vector.scalar_tensor_tensor(wl[:, i * 2 + u], raw[:, u], W_SCALE, wh[:, i * 2 + u], ALU.mult,
                                                       ALU.subtract).then_inc(wl_ready, 1)
                dve.wait_ge(consts, 64)

                def top4(t):
                    dve.wait_ge(ex_done, t + 1)
                    dve.wait_ge(lg_ready, t + 1)
                    nc.vector.scalar_tensor_tensor(lg[:], pt[:, 0:E], 1.0 / X_SCALE, br[:], ALU.mult, ALU.add).then_inc(lg_used, 1)
                    dve.drain()
                    nc.vector.max(mv[:], lg[:])
                    dve.drain()
                    nc.vector.max_index(ixu[:], mv[:], lg[:])
                    nc.vector.tensor_scalar(nm[:], mv[:, 0:1], -1.0, None, ALU.mult).then_inc(top_ready, 1)
                    dve.drain()
                    nc.vector.tensor_copy(ixf[:], ixu[:, 0:TOPK])
                    dve.drain()
                    nc.vector.tensor_copy(ix_all[:, t], ixf[:])
                    for k in range(TOPK):
                        nc.vector.tensor_scalar(oh[:, k], iota[:], ixf[:, k:k + 1], None, ALU.is_equal)

                def weights(t):
                    dve.wait_ge(ex_done, t + 2)
                    nc.vector.reciprocal(rs[:], se[:])
                    dve.drain()
                    nc.vector.tensor_scalar(wk[:], ex[:], rs[:], None, ALU.mult)
                    nc.vector.tensor_reduce(M_all[:, t], oh[:].rearrange("p k e -> p e k"), AX.X, ALU.add)
                    dve.drain()
                    nc.vector.tensor_copy(w_all[:, t], wk[:])
                    nc.vector.tensor_tensor(ohw[:], oh[:], wk[:].unsqueeze(2).to_broadcast([P, TOPK, E]), ALU.mult)
                    dve.drain()
                    nc.vector.tensor_reduce(Wd_all[:, t], ohw[:].rearrange("p k e -> p e k"), AX.X, ALU.add)
                    dve.drain()

                def merged(n, m):
                    dve.wait_ge(br_ready, n * 4 + m + 1)
                    ga, gb = sg[:, 2 * m:2 * m + 2], sg[:, 8 + 2 * m:8 + 2 * m + 2]
                    nc.vector.scalar_tensor_tensor(t1[:], pa[m % 2][:], 1.0 / W_SCALE, ga, ALU.mult, ALU.mult)
                    nc.vector.scalar_tensor_tensor(t2[:], pb[m % 2][:], 1.0 / W_SCALE, gb, ALU.mult, ALU.mult).then_inc(br_used, 1)
                    dve.drain()
                    nc.vector.tensor_tensor(t1[:], t1[:], t2[:], ALU.add).then_inc(m_ready, 1)
                    dve.wait_ge(mh_ready, n * 4 + m + 1)
                    nc.vector.tensor_tensor(ml[:, 2 * m:2 * m + 2], t1[:], mh[:, 2 * m:2 * m + 2], ALU.subtract).then_inc(ml_ready, 1)
                    dve.drain()

                def normed(t, b, c):
                    dve.wait_ge(po_ready, t + 2)
                    dve.wait_ge(hi_ready, t + 1)
                    dve.wait_ge(tr_ready, t + 1)
                    nc.vector.tensor_tensor(h2[:, c], po[:], rows[:, 0], ALU.mult).then_inc(po_used, 1)
                    dve.drain()
                    nc.vector.tensor_tensor(x[:, b, c], h2[:, c], x[:, b, c], ALU.add).then_inc(x1_ready, 1)
                    dve.drain()
                    dve.wait_ge(rstd_ready, t + 3)
                    nc.vector.scalar_tensor_tensor(h2[:, c], x[:, b, c], rstd[:, c:c + 1], rows[:, 1], ALU.mult, ALU.mult)
                    dve.drain()
                    nc.vector.tensor_tensor(h2[:, c], h2[:, c], rows[:, 2], ALU.add).then_inc(h2_ready, 1)

                def low(t, c):
                    dve.wait_ge(hi_ready, t + 3)
                    nc.vector.tensor_tensor(hl[:, c, 1], h2[:, c], hl[:, c, 0], ALU.subtract).then_inc(hl_ready, 1)

                def body(n, b, i):
                    t = n * 2
                    if i is not None:
                        normed(t - 1, 1 - b, 1)
                    dve.wait_ge(sg_in, n * 16 + 16)
                    merged(n, 0)
                    if i is not None:
                        low(t - 1, 1)
                        top4(t - 2)
                    merged(n, 1)
                    if i is not None:
                        weights(t - 2)
                    merged(n, 2)
                    if i is not None:
                        top4(t - 1)
                    merged(n, 3)
                    if i is not None:
                        weights(t - 1)
                    dve.wait_ge(x_in[b], 16 if i is None else x_count(i, b))
                    if i is None:
                        dve.wait_ge(rows_in, 48)
                    else:
                        dve.wait_ge(rows2_in, 48)
                    normed(t, b, 0)
                    low(t, 0)
                dve.sem_inc(hi_ready, 2)
                groups(dve, body)
                normed(NT - 1, LAST_B, 1)
                low(NT - 1, 1)
                for t in (NT - 2, NT - 1):
                    top4(t)
                    weights(t)

            @block.tensor
            def _(pe):
                pe.sem_inc(po_ready, 1)
                pe.sem_inc(tr_ready, 2)
                pe.wait_ge(wl_ready, 2 + 8)
                pe.wait_ge(consts, 64)

                def transposes(t, c):
                    pe.wait_ge(h2_ready, t + 3)
                    pe.wait_ge(lg_used, t + 1)
                    for j in range(KD):
                        mm = nc.tensor.transpose(pt[:, bass.ts(j, P)], h2[:, c, bass.ts(j, P)], ident[:])
                    mm.then_inc(tr_ready, 1)

                def logits(t):
                    pe.wait_ge(hT_ready, t + 2)
                    for k in range(KD):
                        mm = nc.tensor.matmul(pt[:, 0:E], hT[:, k], wr[:, k], start=(k == 0), stop=(k == KD - 1))
                    mm.then_inc(lg_ready, 1)

                def branches(n, m, b):
                    pe.wait_ge(br_used, n * 4 + m + 1)
                    for half in range(2):
                        cols = bass.ts(2 * m + half, P)
                        for dst, w0, y0 in ((pa, 0, 0), (pb, 4, 8)):
                            for k in range(4):
                                yh, yl = yin[:, b, y0 + k], yin[:, b, y0 + 4 + k]
                                nc.tensor.matmul(dst[m % 2][:, half], wh[:, w0 + k, cols], yh, start=(k == 0), stop=False)
                                nc.tensor.matmul(dst[m % 2][:, half], wh[:, w0 + k, cols], yl, start=False, stop=False)
                                mm = nc.tensor.matmul(dst[m % 2][:, half], wl[:, w0 + k, cols], yh, start=False, stop=(k == 3))
                    mm.then_inc(br_ready, 1)

                def body(n, b, i):
                    t = n * 2
                    pe.wait_ge(y_in[b], 16 if i is None else x_count(i, b))
                    branches(n, 0, b)
                    if i is not None:
                        logits(t - 2)
                    branches(n, 1, b)
                    if i is not None:
                        transposes(t - 1, 1)
                    branches(n, 2, b)
                    if i is not None:
                        logits(t - 1)
                    branches(n, 3, b)
                    if i is None:
                        pe.wait_ge(wl_ready, 2 + 16)
                    for c in range(2):
                        pe.wait_ge(po_used, t + c + 1)
                        for k in range(KD):
                            if k % 2 == 0:
                                pe.wait_ge(ml_ready, n * 4 + k // 2 + 2)
                            th, tl = mh[:, k, bass.ts(c, P)], ml[:, k, bass.ts(c, P)]
                            for q in range(2):
                                cols = bass.ts(q, 512)
                                nc.tensor.matmul(po[:, cols], th, wh[:, 8 + k, cols], start=(k == 0), stop=False)
                                nc.tensor.matmul(po[:, cols], th, wl[:, 8 + k, cols], start=False, stop=False)
                                mm = nc.tensor.matmul(po[:, cols], tl, wh[:, 8 + k, cols], start=False, stop=(k == KD - 1))
                        mm.then_inc(po_ready, 1)
                    transposes(t, 0)
                groups(pe, body)
                logits(NT - 2)
                transposes(NT - 1, 1)
                logits(NT - 1)


def stage_dispatch(nc, io, keep):
    Q = NT * TOPK
    with ExitStack() as ctx:
        sb = lambda n, s, d=F32: ctx.enter_context(nc.sbuf_tensor(n, s, d))
        sem = nc.alloc_semaphore
        tri, ones, iota = sb("d_tri", [P, P]), sb("d_ones", [P, P]), sb("d_iota", [P, P])
        pair, spare = sb("d_pair", [P, Q]), sb("d_spare", [P, 1])
        before, G = sb("d_before", [P, NT + 1, E]), sb("d_G", [P, NT, E])
        oh = sb("d_oh", [P, NT, E])
        cnt_i, nb, incl, base = sb("d_cnt", [P, E], I32), sb("d_nb", [P, E]), sb("d_incl", [P, E]), sb("d_base", [P, E])
        one_row = sb("d_one", [P, E])
        pos, pos_i = sb("d_pos", [P, NT, TOPK]), sb("d_posi", [P, 3, Q], I32)
        row_f, blk_f = sb("d_row", [P, Q]), sb("d_blk", [P, Q])
        ohr, ohb, zero = sb("d_ohr", [P, 2, P]), sb("d_ohb", [P, 2, MAX_BLOCKS]), sb("d_zero", [P, P])
        tab, taz = sb("d_tab", [P, MAX_BLOCKS + 1]), sb("d_taz", [P, MAX_BLOCKS + 1])
        cps = ctx.enter_context(nc.psum_tensor("d_cps", [P, 2, 512], F32))
        rps = ctx.enter_context(nc.psum_tensor("d_rps", [P, 2, 512], F32))
        tps = ctx.enter_context(nc.psum_tensor("d_tps", [P, 512], F32))
        consts, counted, oh_ready, oh_used, tab_ready = sem("d_consts"), sem("d_counted"), sem("d_oh_r"), sem("d_oh_u"), sem("d_tab_r")
        H = NT // 2
        M_all, ix_all = keep["M_all"], keep["ix_all"]
        with nc.Block() as block:

            @block.sync
            def _(sp):
                for dst, src in ((tri, io["tri"]), (iota, io["iota"].partition_broadcast(P)), (pair, io["pair"]), (spare, io["spare"])):
                    sp.dma_start(dst[:], src).then_inc(consts, 16)

            @block.tensor
            def _(pe):
                pe.wait_ge(consts, 64)
                pe.wait_ge(oh_used, 1)
                for n in range(2):
                    m = M_all[:, n * H:(n + 1) * H].rearrange("p t e -> p (t e)")
                    nc.tensor.matmul(cps[:, n, 0:H * E], ones[:], m, start=True, stop=True)
                    mm = nc.tensor.matmul(rps[:, n, 0:H * E], tri[:], m, start=True, stop=True)
                mm.then_inc(counted, 1)
                pe.sem_inc(tab_ready, 2)
                nc.tensor.matmul(tps[:, 0:MAX_BLOCKS], zero[:], zero[:, 0:MAX_BLOCKS], start=True, stop=False)
                with pe.Fori(0, Q // 2) as i:
                    for u in range(2):
                        pe.wait_ge(oh_ready, i * 2 + u + 1)
                        nc.tensor.matmul(tps[:, 0:MAX_BLOCKS], ohr[:, u], ohb[:, u], start=False, stop=False).then_inc(tab_ready, 1)
                nc.tensor.matmul(tps[:, 0:MAX_BLOCKS], zero[:], zero[:, 0:MAX_BLOCKS], start=False, stop=True).then_inc(tab_ready, 1)

            @block.vector
            def _(dve):
                nc.vector.memset(ones[:], 1.0)
                nc.vector.memset(one_row[:], 1.0)
                nc.vector.memset(zero[:], 0.0)
                nc.vector.memset(before[:, 0], 0.0)
                nc.vector.memset(tab[:], 0.0)
                dve.drain()
                dve.sem_inc(oh_used, 1)
                dve.wait_ge(counted, 1)
                for n in range(2):
                    with dve.Fori(0, H) as i:
                        nc.vector.tensor_tensor(before[:, i + (n * H + 1)], before[:, i + n * H], cps[:, n, bass.ts(i, E)], ALU.add)
                        dve.drain()
                nc.vector.tensor_scalar(base[:], before[:, NT], float(P - 1), None, ALU.add)
                dve.drain()
                nc.vector.tensor_copy(cnt_i[:], base[:])
                dve.drain()
                nc.vector.tensor_scalar(cnt_i[:], cnt_i[:], 7, None, ALU.logical_shift_right)
                dve.drain()
                nc.vector.tensor_copy(nb[:], cnt_i[:])
                dve.drain()
                nc.vector.tensor_scalar(nb[:], nb[:], 1.0, None, ALU.max)
                dve.drain()
                nc.vector.tensor_tensor_scan(incl[:], one_row[:], nb[:], 0.0, ALU.mult, ALU.add)
                dve.drain()
                nc.vector.tensor_tensor(base[:], incl[:], nb[:], ALU.subtract)
                dve.drain()
                nc.vector.tensor_scalar(nb[:], incl[:], -1.0, None, ALU.add)
                dve.drain()
                nc.vector.tensor_copy(keep["blocks"][:, 0], base[:])
                nc.vector.tensor_copy(keep["blocks"][:, 1], nb[:])
                dve.drain()
                nc.vector.tensor_scalar(base[:], base[:], float(P), None, ALU.mult)
                dve.drain()
                for n in range(2):
                    nc.vector.tensor_tensor(G[:, n * H:(n + 1) * H], before[:, n * H:(n + 1) * H],
                                            rps[:, n, 0:H * E].rearrange("p (t e) -> p t e", e=E), ALU.add)
                dve.drain()
                nc.vector.tensor_tensor(G[:], G[:], base[:].unsqueeze(1).to_broadcast([P, NT, E]), ALU.add)
                dve.drain()
                for k in range(TOPK):
                    nc.vector.tensor_tensor(oh[:], iota[:, 0:E].unsqueeze(1).to_broadcast([P, NT, E]),
                                            ix_all[:, :, k:k + 1].to_broadcast([P, NT, E]), ALU.is_equal)
                    dve.drain()
                    nc.vector.tensor_tensor(oh[:], oh[:], G[:], ALU.mult)
                    dve.drain()
                    nc.vector.tensor_reduce(pos[:, :, k], oh[:], AX.X, ALU.add)
                    dve.drain()
                nc.vector.tensor_copy(pos_i[:, 0], pos[:].rearrange("p t k -> p (t k)"))
                dve.drain()
                nc.vector.tensor_scalar(pos_i[:, 1], pos_i[:, 0], P - 1, None, ALU.bitwise_and)
                nc.vector.tensor_scalar(pos_i[:, 2], pos_i[:, 0], 7, None, ALU.logical_shift_right)
                dve.drain()
                nc.vector.tensor_copy(row_f[:], pos_i[:, 1])
                nc.vector.tensor_copy(blk_f[:], pos_i[:, 2])
                dve.drain()
                with dve.Fori(0, Q // 2) as i:
                    for u in range(2):
                        q = bass.ds(i * 2 + u, 1)
                        dve.wait_ge(tab_ready, i * 2 + u + 1)
                        nc.vector.tensor_scalar(ohr[:, u], iota[:], row_f[:, q], None, ALU.is_equal)
                        nc.vector.tensor_scalar(ohb[:, u], iota[:, 0:MAX_BLOCKS], blk_f[:, q], pair[:, q], ALU.is_equal, ALU.mult
                                                ).then_inc(oh_ready, 1)
                dve.wait_ge(tab_ready, Q + 3)
                nc.vector.tensor_copy(tab[:, 0:MAX_BLOCKS], tps[:, 0:MAX_BLOCKS])
                dve.drain()
                nc.vector.tensor_scalar(taz[:], tab[:], 0.0, spare[:], ALU.is_equal, ALU.mult)
                dve.drain()
                nc.vector.scalar_tensor_tensor(tab[:], tab[:], -1.0, taz[:], ALU.add, ALU.add)
                dve.drain()
                nc.vector.tensor_copy(keep["dst"][:], tab[:])
                nc.vector.tensor_scalar(taz[:], tab[:], float(TOPK * T - 1), None, ALU.min)
                dve.drain()
                nc.vector.tensor_copy(keep["tok"][:], taz[:])
                dve.drain()
                nc.vector.tensor_scalar(keep["tok"][:], keep["tok"][:], 2, None, ALU.logical_shift_right)
                dve.drain()


RING = 6
CHUNKS = 12
def stage_experts(nc, io, keep):
    F = D
    with ExitStack() as ctx:
        sb = lambda n, s, d=F32: ctx.enter_context(nc.sbuf_tensor(n, s, d))
        sem = nc.alloc_semaphore
        raw = sb("e_raw", [P, RING, 2048])
        w1h, w1l = sb("e_w1h", [P, 4, KD, 512], F16), sb("e_w1l", [P, 4, KD, 512], F16)
        w2h, w2l = sb("e_w2h", [P, KD, D], F16), sb("e_w2l", [P, KD, D], F16)
        bias, bias_hl, sel = sb("e_bias", [2 * E, 2 * F]), sb("e_bias_hl", [2 * E, 2 * F], F16), sb("e_sel", [2 * E, E], F16)
        idb = sb("e_idb", [P, P], F16)
        xraw, xT = sb("e_xraw", [P, 2 * D], F16), sb("e_xT", [P, 2 * KD, P], F16)
        gt, ut, sg, a = (sb(f"e_{n}", [P, 512]) for n in ("gt", "ut", "sg", "a"))
        ahl = sb("e_ahl", [P, 2, 2, 512], F16)
        aT = sb("e_aT", [P, 2, 8, P], F16)
        out = sb("e_out", [P, D])
        tcur, dcur = sb("e_tcur", [P, 1], I32), sb("e_dcur", [P, 1], I32)
        pg = [ctx.enter_context(nc.psum_tensor(f"e_pg{n}", [P, 512], F32)) for n in range(4)]
        po = ctx.enter_context(nc.psum_tensor("e_po", [P, D], F32))
        px = [ctx.enter_context(nc.psum_tensor(f"e_px{n}", [P, 1024], F16)) for n in range(2)]
        raw_in = [sem(f"e_raw_in{n}") for n in range(RING)]
        consts, bias_h, bias_r = sem("e_consts"), sem("e_bias_h"), sem("e_bias_r")
        wh_ready, wl_ready = sem("e_wh_r"), sem("e_wl_r")
        x_in, x_ready, out_done = sem("e_x_in"), sem("e_x_r"), sem("e_out_done")
        g1 = [sem(f"e_g1_{p}") for p in range(2)]
        g1_used = [sem(f"e_g1u_{p}") for p in range(2)]
        gc, sg_r, a_r, ah_r, al_r = ([sem(f"e_{n}{p}") for p in range(2)] for n in ("gc", "sgr", "ar", "ahr", "alr"))
        ta, aT_r = [sem(f"e_ta{p}") for p in range(2)], [sem(f"e_aTr{p}") for p in range(2)]
        tx, xT_r = [sem(f"e_tx{p}") for p in range(2)], [sem(f"e_xTr{p}") for p in range(2)]
        d0, g2, g2_used, out_free = sem("e_d0"), sem("e_g2"), sem("e_g2u"), sem("e_out_free")
        tick_p, tick_pe = sem("e_tick_p"), sem("e_tick_pe")
        blocks = keep["blocks"]
        flatk = lambda t, p: t[:, p].rearrange("p k t -> p (k t)")

        def experts(eng, step):
            def one(e, nxt):
                first = eng.value_load(blocks[0:1, 0, bass.ds(e, 1)], min_val=0, max_val=MAX_BLOCKS - 1)
                last = eng.value_load(blocks[0:1, 1, bass.ds(e, 1)], min_val=0, max_val=MAX_BLOCKS - 1)
                with eng.If(first < last):
                    with eng.Fori(first, last) as B:
                        step(B, e, e)
                step(last, e, nxt)

            with eng.Fori(0, E - 1) as e:
                one(e, e + 1)
            one(E - 1, None)

        def w_part(c, high):
            if c < 8:
                t = w1h if high else w1l
                return t[:, c // 2, (c % 2) * 4:(c % 2) * 4 + 4].rearrange("p k n -> p (k n)")
            t = w2h if high else w2l
            return t[:, 2 * (c - 8):2 * (c - 8) + 2].rearrange("p k n -> p (k n)")

        with nc.Block() as blk:

            @blk.sync
            def _(sp):
                sp.dma_start(idb[:], io["ident16"]).then_inc(consts, 16)
                sp.dma_start(sel[:], io["expert_select"]).then_inc(consts, 16)
                for half in range(2):
                    sp.dma_start(bias[half * E:(half + 1) * E], io["b_gate_up"]).then_inc(consts, 16)

                def load(e, c):
                    sp.wait_ge(wl_ready, e * CHUNKS + c + 1)
                    if c < 8:
                        src = io["w_gate_up"][bass.ds(e * 8 + c, 1)].rearrange("o p n -> (o p) n")
                    else:
                        src = io["w_down"][bass.ds(e * 4 + c - 8, 1)].rearrange("o p n -> (o p) n")
                    sp.dma_start(raw[:, c % RING], src).then_inc(raw_in[c % RING], 16)
                with sp.Fori(0, E) as e:
                    for c in range(CHUNKS):
                        load(e, c)

            @blk.gpsimd
            def _(pool):
                total = pool.value_load(blocks[0:1, 1, E - 1:E], min_val=0, max_val=MAX_BLOCKS - 1)

                def gather(B):
                    nc.gpsimd.tensor_copy(tcur[:], keep["tok"][:, bass.ds(B, 1)])
                    pool.drain()
                    pool.indirect_dma_start(xraw[:], None, io["h2"], bass.IndirectOffsetOnAxis(ap=tcur[:], axis=0)).then_inc(x_in, 16)
                gather(0)
                pool.wait_ge(x_in, 16)
                pool.sem_inc(x_ready, 1)
                with pool.Fori(0, total + 1) as B:
                    pool.wait_ge(tx[1], B + 1)
                    gather(B + 1)
                    pool.wait_ge(x_in, B * 16 + 32)
                    pool.sem_inc(x_ready, 1)
                    nc.gpsimd.tensor_copy(dcur[:], keep["dst"][:, bass.ds(B, 1)])
                    pool.drain()
                    pool.wait_ge(g2_used, B + 2)
                    pool.sem_inc(tick_p, 1)
                    pool.indirect_dma_start(io["rows"], bass.IndirectOffsetOnAxis(ap=dcur[:], axis=0), out[:], None).then_inc(out_done, 16)
                    pool.wait_ge(out_done, B * 16 + 16)
                    pool.sem_inc(out_free, 1)

            @blk.scalar
            def _(act):
                def split(e, c):
                    act.wait_ge(raw_in[c % RING], e * 32 + (c // RING) * 16 + 16)
                    nc.scalar.mul(w_part(c, True), raw[:, c % RING], W_SCALE).then_inc(wh_ready, 1)

                def gate(B, p):
                    act.wait_ge(gc[p], B + 1)
                    nc.scalar.activation(sg[:], gt[:], ACT.Sigmoid, scale=ALPHA * DESCALE).then_inc(sg_r[p], 1)
                    act.wait_ge(a_r[p], B + 1)
                    act.wait_ge(ta[p], B + 1)
                    nc.scalar.copy(ahl[:, p, 0], a[:]).then_inc(ah_r[p], 1)

                def act_T(B, p):
                    act.wait_ge(ta[p], B + 2)
                    act.wait_ge(g2, B + 1)
                    nc.scalar.copy(flatk(aT, p), px[p][:]).then_inc(aT_r[p], 1)

                def x_T(B, p):
                    act.wait_ge(tx[p], B + 1)
                    nc.scalar.copy(xT[:, p * KD:(p + 1) * KD].rearrange("p k t -> p (k t)"), px[p][:]).then_inc(xT_r[p], 1)

                def step(B, e, nxt):
                    new = nxt is not None and nxt is not e
                    if new:
                        act.wait_ge(g1[0], B + 1)
                        split(nxt, 0)
                        split(nxt, 1)
                    act_T(B, 0)
                    if new:
                        split(nxt, 2)
                        split(nxt, 3)
                    gate(B, 1)
                    if nxt is not None:
                        act.wait_ge(g1[1], B + 1)
                        x_T(B + 1, 0)
                        x_T(B + 1, 1)
                    if new:
                        for c in (4, 5, 6):
                            split(nxt, c)
                    act_T(B, 1)
                    if new:
                        split(nxt, 7)
                        act.wait_ge(d0, B + 1)
                        split(nxt, 8)
                    if nxt is not None:
                        gate(B + 1, 0)
                    if new:
                        split(nxt, 9)
                    act.wait_ge(g2, B + 2)
                    act.wait_ge(out_free, B + 1)
                    nc.scalar.activation(out[:], po[:], ACT.Copy, scale=DESCALE).then_inc(g2_used, 1)
                    if new:
                        split(nxt, 10)
                        split(nxt, 11)

                act.sem_inc(out_free, 1)
                act.wait_ge(consts, 64)
                nc.scalar.mul(bias_hl[:], bias[:], W_SCALE).then_inc(bias_h, 1)
                for p in range(2):
                    x_T(0, p)
                for c in range(CHUNKS):
                    split(0, c)
                gate(0, 0)
                experts(act, step)

            @blk.vector
            def _(dve):
                def split(e, c):
                    dve.wait_ge(wh_ready, e * CHUNKS + c + 1)
                    nc.vector.scalar_tensor_tensor(w_part(c, False), raw[:, c % RING], W_SCALE, w_part(c, True), ALU.mult,
                                                   ALU.subtract).then_inc(wl_ready, 1)

                def swiglu(B, p):
                    dve.wait_ge(g1[p], B + 1)
                    nc.vector.tensor_scalar(gt[:], pg[2 * p][:], LIMIT / DESCALE, None, ALU.min).then_inc(gc[p], 1)
                    nc.vector.tensor_scalar(ut[:], pg[2 * p + 1][:], LIMIT / DESCALE, -LIMIT / DESCALE, ALU.min, ALU.max
                                            ).then_inc(g1_used[p], 1)
                    dve.drain()
                    nc.vector.scalar_tensor_tensor(ut[:], ut[:], 1.0 / DESCALE, gt[:], ALU.add, ALU.mult)
                    dve.drain()
                    dve.wait_ge(sg_r[p], B + 1)
                    nc.vector.scalar_tensor_tensor(a[:], ut[:], X_SCALE * DESCALE * DESCALE, sg[:], ALU.mult, ALU.mult).then_inc(a_r[p], 1)
                    dve.wait_ge(ah_r[p], B + 1)
                    nc.vector.tensor_tensor(ahl[:, p, 1], a[:], ahl[:, p, 0], ALU.subtract).then_inc(al_r[p], 1)
                    dve.drain()

                def step(B, e, nxt):
                    new = nxt is not None and nxt is not e
                    if new:
                        for c in range(4):
                            split(nxt, c)
                    swiglu(B, 1)
                    if new:
                        for c in range(4, 9):
                            split(nxt, c)
                    if nxt is not None:
                        swiglu(B + 1, 0)
                    if new:
                        for c in range(9, CHUNKS):
                            split(nxt, c)

                dve.sem_inc(wl_ready, RING)
                dve.wait_ge(bias_h, 1)
                nc.vector.scalar_tensor_tensor(bias_hl[E:], bias[E:], W_SCALE, bias_hl[E:], ALU.mult, ALU.subtract).then_inc(bias_r, 1)
                for c in range(CHUNKS):
                    split(0, c)
                swiglu(0, 0)
                experts(dve, step)

            @blk.tensor
            def _(pe):
                def x_transposes(B):
                    pe.wait_ge(x_ready, B + 1)
                    for p in range(2):
                        for k in range(KD):
                            mm = nc.tensor.transpose(px[p][:, bass.ts(k, P)], xraw[:, bass.ts(p * KD + k, P)], idb[:])
                        mm.then_inc(tx[p], 1)

                def up(B, e, n):
                    p = n // 2
                    if n % 2 == 0:
                        pe.wait_ge(wl_ready, e * CHUNKS + 4 * p + 4 + RING)
                        pe.wait_ge(g1_used[p], B + 1)
                    if n == 0:
                        for q in range(2):
                            pe.wait_ge(xT_r[q], B + 1)
                    pe.sem_inc(tick_pe, 1)
                    cols = bass.ds((n % 2) * F + p * 512, 512)
                    nc.tensor.matmul(pg[n][:], sel[:, bass.ds(e, 1)].to_broadcast([2 * E, P]), bias_hl[:, cols], start=True, stop=False)
                    for k in range(KD):
                        nc.tensor.matmul(pg[n][:], xT[:, k], w1h[:, n, k], start=False, stop=False)
                        nc.tensor.matmul(pg[n][:], xT[:, KD + k], w1h[:, n, k], start=False, stop=False)
                        mm = nc.tensor.matmul(pg[n][:], xT[:, k], w1l[:, n, k], start=False, stop=(k == KD - 1))
                    if n % 2:
                        mm.then_inc(g1[p], 1)

                def act_T(B, p):
                    pe.wait_ge(al_r[p], B + 1)
                    for q in range(2):
                        for k in range(4):
                            mm = nc.tensor.transpose(px[p][:, bass.ts(q * 4 + k, P)], ahl[:, p, q, bass.ts(k, P)], idb[:])
                    mm.then_inc(ta[p], 1)

                def down(p, n):
                    cols = bass.ts(n, 512)
                    for k in range(4):
                        wk = 4 * p + k
                        nc.tensor.matmul(po[:, cols], aT[:, p, k], w2h[:, wk, cols], start=(p == 0 and k == 0), stop=False)
                        nc.tensor.matmul(po[:, cols], aT[:, p, 4 + k], w2h[:, wk, cols], start=False, stop=False)
                        mm = nc.tensor.matmul(po[:, cols], aT[:, p, k], w2l[:, wk, cols], start=False, stop=(p == 1 and k == 3))
                    return mm

                def step(B, e, nxt):
                    up(B, e, 2)
                    act_T(B, 0)
                    up(B, e, 3)
                    pe.wait_ge(aT_r[0], B + 1)
                    pe.wait_ge(wl_ready, e * CHUNKS + 10 + RING)
                    pe.wait_ge(g2_used, B + 1)
                    down(0, 0)
                    if nxt is not None:
                        x_transposes(B + 1)
                    down(0, 1).then_inc(d0, 1)
                    if nxt is not None:
                        up(B + 1, nxt, 0)
                    act_T(B, 1)
                    if nxt is not None:
                        up(B + 1, nxt, 1)
                    pe.wait_ge(aT_r[1], B + 1)
                    pe.wait_ge(wl_ready, e * CHUNKS + CHUNKS + RING)
                    down(1, 0)
                    down(1, 1).then_inc(g2, 1)

                for p in range(2):
                    pe.sem_inc(ta[p], 1)
                    pe.sem_inc(g1_used[p], 1)
                pe.sem_inc(g2, 1)
                pe.sem_inc(g2_used, 1)
                pe.wait_ge(consts, 64)
                x_transposes(0)
                pe.wait_ge(bias_r, 1)
                up(0, 0, 0)
                up(0, 0, 1)
                experts(pe, step)


def stage_combine(nc, io, keep):
    with ExitStack() as ctx:
        sb = lambda n, s, d=F32: ctx.enter_context(nc.sbuf_tensor(n, s, d))
        sem = nc.alloc_semaphore
        r, x1 = sb("c_r", [P, 2, TOPK, D]), sb("c_x1", [P, 2, D])
        y, o = sb("c_y", [P, 2, D]), sb("c_o", [P, 2, D])
        g2, fn, bd, ident = sb("c_g2", [P, D]), sb("c_fn", [P, D]), sb("c_bd", [E, D]), sb("c_ident", [P, P])
        wT, junk, wd = sb("c_wT", [E, P]), sb("c_junk", [P, D]), sb("c_wd", [P, 2, E])
        ss, ms, rstd, mhalf = sb("c_ss", [P, 2]), sb("c_ms", [P, 2]), sb("c_rstd", [P, 2]), sb("c_mhalf", [P, 1])
        pt = ctx.enter_context(nc.psum_tensor("c_pt", [P, 512], F32))
        pb = [ctx.enter_context(nc.psum_tensor(f"c_pb{u}", [P, D], F32)) for u in range(2)]
        consts, g2_in, r_in, o_out = sem("c_consts"), sem("c_g2_in"), [sem(f"c_in{u}") for u in range(2)], [sem(f"c_out{u}") for u in range(2)]
        wd_r, wT_p, wT_r, pb_r, y_r, ss_r, rstd_r, o_r = (sem(f"c_{n}") for n in ("wd", "wTp", "wTr", "pbr", "yr", "ssr", "rstdr", "or"))
        tick, o_free = sem("c_tick"), sem("c_o_free")
        w_all, Wd_all = keep["w_all"], keep["Wd_all"]
        mrows = io["mod_rows"].rearrange("(v q k) p -> v q (k p)", v=2, q=4)

        def tiles(eng, body, between=None):
            body(0)
            if between:
                between()
            with eng.Fori(1, NT // 2) as i:
                body(i)

        with nc.Block() as block:

            @block.sync
            def _(sp):
                sp.dma_start(g2[:], mrows[0, 3].partition_broadcast(P)).then_inc(g2_in, 16)
                sp.dma_start(fn[:], io["final_norm"].partition_broadcast(P)).then_inc(consts, 16)
                sp.dma_start(bd[:], io["b_down"]).then_inc(consts, 16)
                sp.dma_start(ident[:], io["ident"]).then_inc(consts, 16)
                for u in range(2):
                    sp.sem_inc(o_out[u], 16)

                def body(i):
                    for u in range(2):
                        t = i * 2 + u
                        sp.wait_ge(y_r, t + 1)
                        sp.dma_start(r[:, u], io["rows"][bass.ts(t, TOPK * P), :].rearrange("(p k) d -> p k d", k=TOPK)).then_inc(r_in[u], 16)
                        sp.dma_start(x1[:, u], io["x1"][bass.ts(t, P), :]).then_inc(r_in[u], 16)
                    for u in range(2):
                        t = i * 2 + u
                        sp.wait_ge(o_r, t + 1)
                        sp.dma_start(io["y"][bass.ts(t, P), :], o[:, u]).then_inc(o_out[u], 16)

                def latent():
                    sp.wait_ge(y_r, 4)
                    sp.dma_start(g2[:], mrows[1, 3].partition_broadcast(P)).then_inc(g2_in, 16)
                tiles(sp, body, latent)
                for u in range(2):
                    sp.wait_ge(o_out[u], 16 * (NT // 2) + 16)

            @block.tensor
            def _(pe):
                pe.wait_ge(consts, 48)
                with pe.Fori(0, NT // 2) as i:
                    for u in range(2):
                        t = i * 2 + u
                        pe.wait_ge(wd_r, t + 1)
                        pe.wait_ge(wT_r, t + 1)
                        nc.tensor.transpose(pt[0:E, 0:P], wd[:, u], ident[:]).then_inc(wT_p, 1)
                        pe.wait_ge(wT_r, t + 2)
                        pe.wait_ge(y_r, t + 1)
                        for n in range(2):
                            mm = nc.tensor.matmul(pb[u][:, bass.ts(n, 512)], wT[:], bd[:, bass.ts(n, 512)], start=True, stop=True)
                        mm.then_inc(pb_r, 1)

            @block.scalar
            def _(act):
                act.sem_inc(wT_r, 1)

                def body(i):
                    for u in range(2):
                        t = i * 2 + u
                        act.wait_ge(wT_p, t + 1)
                        act.wait_ge(pb_r, t + 1)
                        nc.scalar.copy(wT[:], pt[0:E, 0:P]).then_inc(wT_r, 1)
                    for u in range(2):
                        t = i * 2 + u
                        act.wait_ge(y_r, t + 3)
                        act.wait_ge(rstd_r, t + 1)
                        nc.scalar.activation(junk[:], y[:, u], ACT.Square, accum_out=ss[:, u:u + 1]).then_inc(ss_r, 1)
                        act.drain()
                act.sem_inc(pb_r, 1)
                tiles(act, body)

            @block.gpsimd
            def _(pool):
                nc.gpsimd.memset(mhalf[:], -0.5)
                pool.drain()
                pool.sem_inc(rstd_r, 2)

                def body(i):
                    for u in range(2):
                        t = i * 2 + u
                        pool.wait_ge(ss_r, t + 1)
                        pool.wait_ge(o_free, t + 1)
                        pool.sem_inc(tick, 1)
                        nc.gpsimd.tensor_scalar(ms[:, u:u + 1], ss[:, u:u + 1], 1.0 / D, EPS, ALU.mult, ALU.add)
                        pool.drain()
                        nc.gpsimd.tensor_tensor(rstd[:, u:u + 1], ms[:, u:u + 1], mhalf[:], ALU.pow).then_inc(rstd_r, 1)
                tiles(pool, body)

            @block.vector
            def _(dve):
                dve.wait_ge(consts, 48)
                dve.sem_inc(y_r, 2)
                dve.sem_inc(o_free, 2)

                def body(i):
                    for u in range(2):
                        t = i * 2 + u
                        dve.wait_ge(wT_r, t + 1)
                        nc.vector.tensor_copy(wd[:, u], Wd_all[:, t]).then_inc(wd_r, 1)
                    for u in range(2):
                        t = i * 2 + u
                        wk = lambda k: w_all[:, t, k:k + 1]
                        dve.wait_ge(r_in[u], i * 32 + 32)
                        dve.wait_ge(g2_in, 16 if isinstance(i, int) else 32)
                        dve.wait_ge(rstd_r, t + 1)
                        nc.vector.tensor_scalar(y[:, u], r[:, u, 0], wk(0), None, ALU.mult)
                        dve.drain()
                        for k in range(1, TOPK):
                            nc.vector.scalar_tensor_tensor(y[:, u], r[:, u, k], wk(k), y[:, u], ALU.mult, ALU.add)
                            dve.drain()
                        dve.wait_ge(pb_r, t + 2)
                        nc.vector.tensor_tensor(y[:, u], y[:, u], pb[u][:], ALU.add)
                        dve.drain()
                        nc.vector.tensor_tensor(y[:, u], y[:, u], g2[:], ALU.mult)
                        dve.drain()
                        nc.vector.tensor_tensor(y[:, u], y[:, u], x1[:, u], ALU.add).then_inc(y_r, 1)
                    for u in range(2):
                        t = i * 2 + u
                        dve.wait_ge(rstd_r, t + 3)
                        dve.wait_ge(o_out[u], i * 16 + 16)
                        nc.vector.scalar_tensor_tensor(o[:, u], y[:, u], rstd[:, u:u + 1], fn[:], ALU.mult, ALU.mult).then_inc(o_r, 1)
                    dve.drain()
                    dve.sem_inc(o_free, 2)
                tiles(dve, body)


SCRATCH = (
    ("mod_rows", (64, P), F32),
    ("proj", (36 * P, T), F32),
    ("vals", (T, HEADS * P), F32),
    ("yab", (P, 16, T), F16),
    ("x1", (T, D), F32),
    ("h2", (T, 2 * D), F16),
    ("rows", (TOPK * T + P, D), F32),
)


def build(nc, io):
    with ExitStack() as outer:
        osb = lambda n, s, d=F32: outer.enter_context(nc.sbuf_tensor(n, s, d))
        keep = {"A1": osb("A1", [P, 2, KD]), "B1": osb("B1", [P, 2, KD]), "lb": osb("lb", [P, 8]), "oml": osb("oml", [P, 8])}
        with nc.cleanup_on_exit():
            stage_modulation(nc, io, keep)
        with ExitStack() as b:
            keep["hT_hi"] = b.enter_context(nc.sbuf_tensor("hT_hi", [P, KD, T], F16))
            keep["hT_lo"] = b.enter_context(nc.sbuf_tensor("hT_lo", [P, KD, T], F16))
            with nc.cleanup_on_exit():
                stage_normed(nc, io, keep)
            with nc.cleanup_on_exit():
                stage_projection(nc, io, keep)
        with ExitStack() as a:
            keep["oT"] = [a.enter_context(nc.sbuf_tensor(f"oT{r}", [P, HEADS, T], F32)) for r in range(2)]
            with nc.cleanup_on_exit():
                stage_scan(nc, io, keep)
            with nc.cleanup_on_exit():
                stage_hgrn_out(nc, io, keep)
        with nc.cleanup_on_exit():
            stage_pooling(nc, io, keep)
        with ExitStack() as a:
            for n in ("M_all", "Wd_all"):
                keep[n] = a.enter_context(nc.sbuf_tensor(n, [P, NT, E], F32))
            for n in ("ix_all", "w_all"):
                keep[n] = a.enter_context(nc.sbuf_tensor(n, [P, NT, TOPK], F32))
            with nc.cleanup_on_exit():
                stage_merge(nc, io, keep)
            keep["blocks"] = a.enter_context(nc.sbuf_tensor("blocks", [P, 2, E], I32))
            keep["dst"] = a.enter_context(nc.sbuf_tensor("dst", [P, MAX_BLOCKS + 1], I32))
            keep["tok"] = a.enter_context(nc.sbuf_tensor("tok", [P, MAX_BLOCKS + 1], I32))
            with nc.cleanup_on_exit():
                stage_dispatch(nc, io, keep)
            with nc.cleanup_on_exit():
                stage_experts(nc, io, keep)
            with nc.cleanup_on_exit():
                stage_combine(nc, io, keep)


def shape_constants(np):
    p = np.arange(P)
    same = (p[:, None] // CHUNK) == (p[None] // CHUNK)
    col = np.arange(HEADS * P)

    def inverse_counts(n, w):
        at = np.arange(n)
        first, last = np.clip(at - w // 2, 0, n - 1), np.clip(at - w // 2 + w - 1, 0, n - 1)
        return 1.0 / (last - first + 1)

    pairs = (p[:, None, None] + P * np.arange(NT)[None, :, None]) * TOPK + np.arange(TOPK) + 1
    return {
        "ident": np.eye(P, dtype=np.float32),
        "ident16": np.eye(P, dtype=np.float16),
        "mask_f": np.tile((same & (p[:, None] <= p[None])).astype(np.uint32), (1, HEADS)),
        "mask_b": np.tile((same & (p[:, None] >= p[None])).astype(np.uint32), (1, HEADS)),
        "reset_f": np.tile((col % CHUNK != 0).astype(np.float32), (P, 1)),
        "reset_b": np.tile((col % CHUNK != CHUNK - 1).astype(np.float32), (P, 1)),
        "pool_inv": np.stack([np.concatenate([inverse_counts(n, w) for n in (GRID_H, GRID_W, CTX)])
                              for w in WINDOWS]).astype(np.float32),
        "expert_select": np.tile(X_SCALE * np.eye(E), (2, 1)).astype(np.float16),
        "iota": p.astype(np.float32),
        "tri": (p[:, None] < p[None]).astype(np.float32),
        "pair": pairs.reshape(P, NT * TOPK).astype(np.float32),
        "spare": (TOPK * T + 1 + p)[:, None].astype(np.float32),
    }


def kernel(**inputs):
    import numpy as np
    import concourse.bacc as bacc
    from concourse.bass_utils import run_bass_kernel_spmd

    a = {name: np.asarray(value) for name, value in inputs.items()}

    def column(v):
        return v.reshape(-1, P).transpose(1, 0)

    w_in = a["w_in"][0].reshape(KD, P, NCOL, P).transpose(2, 1, 0, 3)
    state = a["state_hgrn"][0, 0].transpose(0, 2, 1, 3).reshape(2, P, HEADS * P)
    arrays = {
        "x": np.concatenate([a["x_prompt"][0], a["x_sample"][0]]),
        "cc": np.stack([a["c_ctx"], a["c"][0]]).reshape(2, KD, P).transpose(2, 1, 0),
        "w_ada": a["w_ada"][0],
        "b_ada_c": column(a["b_ada"][0]),
        "norm1_c": column(a["norm1"][0]),
        "norm2_c": column(a["norm2"][0]),
        "lb_c": a["hgrn_lb"].reshape(2, 2 * HEADS, P).transpose(2, 0, 1),
        "w_in": np.concatenate([w_in[0:12], w_in[16:40], w_in[12:16]]),
        "state_f": state[0],
        "state_b": state[1],
        "hgrn_norm_c": column(a["hgrn_norm"][0]),
        "w_pool_l": a["w_pool"][0].transpose(1, 0, 2),
        "pool_scale_c": column(a["pool_scale"][0]),
        "w_merge": np.concatenate([a["w_branch_a"][0], a["w_branch_b"][0], a["w_out"][0]]),
        "w_router_l": a["w_router"][0].reshape(KD, P, E).transpose(1, 0, 2),
        "b_router": a["b_router"][0],
        "w_gate_up": a["w_gate_up"][0].reshape(E, 2, 4, P, 2, 2, 512).transpose(0, 5, 4, 1, 3, 2, 6).reshape(8 * E, P, 2048),
        "w_down": a["w_down"][0].reshape(E, 4, 2, P, D).transpose(0, 1, 3, 2, 4).reshape(4 * E, P, 2048),
        "b_gate_up": a["b_gate_up"][0],
        "b_down": a["b_down"][0],
        "final_norm": a["final_norm"],
    }
    arrays.update(shape_constants(np))
    arrays = {name: np.ascontiguousarray(value) for name, value in arrays.items()}

    nc = bacc.Bacc("TRN2", target_bir_lowering=False, num_devices=1)
    io = {name: nc.dram_tensor(name, value.shape, mybir.dt.from_np(value.dtype), kind="ExternalInput").ap()
          for name, value in arrays.items()}
    for name, shape, dtype in SCRATCH:
        io[name] = nc.dram_tensor(name, shape, dtype, kind="Internal").ap()
    for name, shape in (("y", (T, D)), ("new_state", (2, HEADS, P, P))):
        io[name] = nc.dram_tensor(name, shape, F32, kind="ExternalOutput").ap()
    build(nc, io)
    out = run_bass_kernel_spmd(nc, [arrays], core_ids=[0]).results[0]
    y = out["y"]
    return y[None, :CTX], y[None, CTX:], out["new_state"].reshape(1, 1, 2, HEADS, P, P)
```
